# Optimizing a Trainium2 kernel written in Bass

```python
import jax
import jax.numpy as jnp
from jax import lax
import numpy as np

D_MODEL = 1024
BATCH = 1
SEQ = 1024
DEPTH = 2

N_MIXERS = 3
NORM_EPS = 1e-6
ROPE_THETA = 10000.0

RET_HEADS = 4
RET_QK_DIM = D_MODEL // RET_HEADS
RET_V_DIM = 2 * D_MODEL // RET_HEADS
RET_CHUNK = 128

LRU_WIDTH = -(-(4 * D_MODEL // 3) // 256) * 256
LRU_BLOCKS = 8
LRU_BLOCK_W = LRU_WIDTH // LRU_BLOCKS
LRU_C = 8.0
CONV_WIDTH = 4

SWA_HEAD_DIM = 64
SWA_Q_HEADS = D_MODEL // SWA_HEAD_DIM
SWA_KV_HEADS = 4
SWA_GROUP = SWA_Q_HEADS // SWA_KV_HEADS
SWA_WINDOW = 128
SWA_BLOCK = 128

FFN_HIDDEN = -(-(8 * D_MODEL // 3) // 256) * 256

N_RET = len(range(0, DEPTH, N_MIXERS))
N_LRU = len(range(1, DEPTH, N_MIXERS))
N_SWA = len(range(2, DEPTH, N_MIXERS))

kernel_name = 'hybrid_retention_rglru_swa_sink_decoder'

def rms_norm(x, gain):
    xf = x.astype(jnp.float32)
    y = xf * lax.rsqrt(jnp.mean(xf * xf, axis=-1, keepdims=True) + NORM_EPS)
    return (y * gain.astype(jnp.float32)).astype(x.dtype)

def apply_rope(t, positions):
    dh = t.shape[-1]
    half = dh // 2
    inv_freq = ROPE_THETA ** (-jnp.arange(half, dtype=jnp.float32) * 2.0 / dh)
    ang = positions.astype(jnp.float32)[..., None] * inv_freq
    cos = jnp.cos(ang)[:, :, None, :]
    sin = jnp.sin(ang)[:, :, None, :]
    tf = t.astype(jnp.float32)
    t1, t2 = tf[..., :half], tf[..., half:]
    return jnp.concatenate([t1 * cos - t2 * sin, t2 * cos + t1 * sin], axis=-1).astype(t.dtype)

def retention(h, positions, w_in, w_out):
    B, S, _ = h.shape
    H, dk, dv, C = RET_HEADS, RET_QK_DIM, RET_V_DIM, RET_CHUNK
    nc = S // C
    q, k, v, g = jnp.split(h @ w_in, [H * dk, 2 * H * dk, 2 * H * dk + H * dv], axis=-1)
    q = apply_rope(q.reshape(B, S, H, dk), positions)
    k = apply_rope(k.reshape(B, S, H, dk), positions) * (dk ** -0.5)
    v = v.reshape(B, S, H, dv)

    def to_chunks(t):
        return t.reshape(B, nc, C, H, t.shape[-1]).transpose(1, 0, 3, 2, 4)

    log_gamma = jnp.log1p(-(2.0 ** (-5.0 - jnp.arange(H, dtype=jnp.float32))))
    idx = jnp.arange(C, dtype=jnp.float32)
    rel = idx[:, None] - idx[None, :]
    intra = jnp.where(rel >= 0, jnp.exp(jnp.maximum(rel, 0.0) * log_gamma[:, None, None]), 0.0).astype(h.dtype)
    q_decay = jnp.exp((idx + 1.0)[None, :] * log_gamma[:, None]).astype(h.dtype)
    k_decay = jnp.exp((C - 1.0 - idx)[None, :] * log_gamma[:, None]).astype(h.dtype)
    chunk_decay = jnp.exp(C * log_gamma).astype(h.dtype)

    def step(state, inp):
        qi, ki, vi = inp
        scores = jnp.einsum('bhqd,bhkd->bhqk', qi, ki) * intra[None]
        o_inner = jnp.einsum('bhqk,bhkv->bhqv', scores, vi)
        o_cross = jnp.einsum('bhqd,bhdv->bhqv', qi, state) * q_decay[None, :, :, None]
        new_state = state * chunk_decay[None, :, None, None] + jnp.einsum(
            'bhkd,bhkv->bhdv', ki * k_decay[None, :, :, None], vi)
        return new_state, o_inner + o_cross

    state0 = jnp.zeros((B, H, dk, dv), h.dtype)
    _, o = lax.scan(step, state0, (to_chunks(q), to_chunks(k), to_chunks(v)))
    o = o.transpose(1, 0, 3, 2, 4).reshape(B, S, H, dv)
    of = o.astype(jnp.float32)
    o = (of * lax.rsqrt(jnp.mean(of * of, axis=-1, keepdims=True) + NORM_EPS)).astype(h.dtype)
    o = o.reshape(B, S, H * dv) * jax.nn.silu(g)
    return o @ w_out

def rglru_block(h, w_in, conv_w, conv_b, w_r, b_r, w_i, b_i, lam, w_out):
    B, S, _ = h.shape
    gate, u = jnp.split(h @ w_in, 2, axis=-1)
    u = lax.conv_general_dilated(
        u, conv_w[:, None, :].astype(u.dtype), window_strides=(1,),
        padding=[(CONV_WIDTH - 1, 0)], dimension_numbers=('NWC', 'WIO', 'NWC'),
        feature_group_count=LRU_WIDTH) + conv_b
    ub = u.reshape(B, S, LRU_BLOCKS, LRU_BLOCK_W)
    r = jax.nn.sigmoid(jnp.einsum('bsnc,ncd->bsnd', ub, w_r) + b_r).reshape(B, S, LRU_WIDTH)
    i = jax.nn.sigmoid(jnp.einsum('bsnc,ncd->bsnd', ub, w_i) + b_i).reshape(B, S, LRU_WIDTH)
    log_a = (-LRU_C * jax.nn.softplus(-lam.astype(jnp.float32))) * r.astype(jnp.float32)
    a = jnp.exp(log_a)
    b = jnp.sqrt(-jnp.expm1(2.0 * log_a)) * (i * u).astype(jnp.float32)

    def combine(left, right):
        a_l, b_l = left
        a_rt, b_rt = right
        return a_l * a_rt, a_rt * b_l + b_rt

    _, hs = lax.associative_scan(combine, (a, b), axis=1)
    y = hs.astype(h.dtype) * jax.nn.gelu(gate)
    return y @ w_out

def sliding_window_sink_attention(h, positions, w_qkv, b_qkv, sinks, w_out, b_out):
    B, S, _ = h.shape
    Hq, Hkv, G, dh, L = SWA_Q_HEADS, SWA_KV_HEADS, SWA_GROUP, SWA_HEAD_DIM, SWA_BLOCK
    nb = S // L
    q, k, v = jnp.split(h @ w_qkv + b_qkv, [Hq * dh, (Hq + Hkv) * dh], axis=-1)
    q = apply_rope(q.reshape(B, S, Hq, dh), positions) * (dh ** -0.5)
    k = apply_rope(k.reshape(B, S, Hkv, dh), positions)
    v = v.reshape(B, S, Hkv, dh)
    qb = q.reshape(B, nb, L, Hkv, G, dh)
    kb = k.reshape(B, nb, L, Hkv, dh)
    vb = v.reshape(B, nb, L, Hkv, dh)

    def with_prev(t):
        prev = jnp.concatenate([jnp.zeros_like(t[:, :1]), t[:, :-1]], axis=1)
        return jnp.concatenate([prev, t], axis=2)

    kw, vw = with_prev(kb), with_prev(vb)
    scores = jnp.einsum('bnqkgd,bnskd->bnkgqs', qb, kw).astype(jnp.float32)
    qi = jnp.arange(L)[:, None]
    si = jnp.arange(2 * L)[None, :]
    dist = qi + L - si
    in_window = (dist >= 0) & (dist < SWA_WINDOW)
    has_key = (jnp.arange(nb)[:, None, None] > 0) | (si[None] >= L)
    mask = in_window[None] & has_key
    scores = jnp.where(mask[None, :, None, None], scores, -jnp.inf)
    sink = jnp.broadcast_to(sinks.astype(jnp.float32).reshape(1, 1, Hkv, G, 1, 1), scores.shape[:-1] + (1,))
    probs = jax.nn.softmax(jnp.concatenate([scores, sink], axis=-1), axis=-1)[..., :-1].astype(h.dtype)
    o = jnp.einsum('bnkgqs,bnskd->bnqkgd', probs, vw).reshape(B, S, Hq * dh)
    return o @ w_out + b_out

def swiglu_ffn(h, w_gu, w_down):
    gate, up = jnp.split(h @ w_gu, 2, axis=-1)
    return (jax.nn.silu(gate) * up) @ w_down

def setup_inputs(seed: int = 0) -> dict:
    key = jax.random.key(seed)
    ks = jax.random.split(key, 24)
    f32 = jnp.float32

    def dense(k, shape, fan_in):
        return jax.random.normal(k, shape, f32) * (fan_in ** -0.5)

    def small(k, shape, scale):
        return scale * jax.random.normal(k, shape, f32)

    x = jax.random.normal(ks[0], (BATCH, SEQ, D_MODEL), f32)
    start = jax.random.randint(ks[1], (BATCH, 1), 0, SEQ, dtype=jnp.int32)
    positions = start + jnp.arange(SEQ, dtype=jnp.int32)[None, :]
    mix_norm = 1.0 + small(ks[2], (DEPTH, D_MODEL), 0.02)
    ffn_norm = 1.0 + small(ks[3], (DEPTH, D_MODEL), 0.02)
    final_norm = 1.0 + small(ks[4], (D_MODEL,), 0.02)

    ret_in_dim = 2 * RET_HEADS * RET_QK_DIM + 2 * RET_HEADS * RET_V_DIM
    ret_w_in = dense(ks[5], (N_RET, D_MODEL, ret_in_dim), D_MODEL)
    ret_w_out = dense(ks[6], (N_RET, RET_HEADS * RET_V_DIM, D_MODEL), RET_HEADS * RET_V_DIM)

    lru_w_in = dense(ks[7], (N_LRU, D_MODEL, 2 * LRU_WIDTH), D_MODEL)
    lru_conv_w = dense(ks[8], (N_LRU, CONV_WIDTH, LRU_WIDTH), CONV_WIDTH)
    lru_conv_b = small(ks[9], (N_LRU, LRU_WIDTH), 0.01)
    lru_w_r = dense(ks[10], (N_LRU, LRU_BLOCKS, LRU_BLOCK_W, LRU_BLOCK_W), LRU_BLOCK_W)
    lru_b_r = small(ks[11], (N_LRU, LRU_BLOCKS, LRU_BLOCK_W), 0.1)
    lru_w_i = dense(ks[12], (N_LRU, LRU_BLOCKS, LRU_BLOCK_W, LRU_BLOCK_W), LRU_BLOCK_W)
    lru_b_i = small(ks[13], (N_LRU, LRU_BLOCKS, LRU_BLOCK_W), 0.1)
    a_pow_c = jax.random.uniform(ks[14], (N_LRU, LRU_WIDTH), f32, 0.9, 0.999)
    a_base = a_pow_c ** (1.0 / LRU_C)
    lru_lambda = jnp.log(a_base) - jnp.log1p(-a_base)
    lru_w_out = dense(ks[15], (N_LRU, LRU_WIDTH, D_MODEL), LRU_WIDTH)

    qkv_dim = (SWA_Q_HEADS + 2 * SWA_KV_HEADS) * SWA_HEAD_DIM
    swa_w_qkv = dense(ks[16], (N_SWA, D_MODEL, qkv_dim), D_MODEL)
    swa_b_qkv = small(ks[17], (N_SWA, qkv_dim), 0.01)
    swa_sinks = small(ks[18], (N_SWA, SWA_Q_HEADS), 0.5)
    swa_w_out = dense(ks[19], (N_SWA, SWA_Q_HEADS * SWA_HEAD_DIM, D_MODEL), SWA_Q_HEADS * SWA_HEAD_DIM)
    swa_b_out = small(ks[20], (N_SWA, D_MODEL), 0.01)

    ffn_w_gu = dense(ks[21], (DEPTH, D_MODEL, 2 * FFN_HIDDEN), D_MODEL)
    ffn_w_down = dense(ks[22], (DEPTH, FFN_HIDDEN, D_MODEL), FFN_HIDDEN)

    return {'x': x, 'positions': positions, 'mix_norm': mix_norm, 'ffn_norm': ffn_norm,
            'final_norm': final_norm, 'ret_w_in': ret_w_in, 'ret_w_out': ret_w_out,
            'lru_w_in': lru_w_in, 'lru_conv_w': lru_conv_w, 'lru_conv_b': lru_conv_b,
            'lru_w_r': lru_w_r, 'lru_b_r': lru_b_r, 'lru_w_i': lru_w_i, 'lru_b_i': lru_b_i,
            'lru_lambda': lru_lambda, 'lru_w_out': lru_w_out, 'swa_w_qkv': swa_w_qkv,
            'swa_b_qkv': swa_b_qkv, 'swa_sinks': swa_sinks, 'swa_w_out': swa_w_out,
            'swa_b_out': swa_b_out, 'ffn_w_gu': ffn_w_gu, 'ffn_w_down': ffn_w_down}

def reference(x, positions, mix_norm, ffn_norm, final_norm, ret_w_in, ret_w_out,
              lru_w_in, lru_conv_w, lru_conv_b, lru_w_r, lru_b_r, lru_w_i, lru_b_i,
              lru_lambda, lru_w_out, swa_w_qkv, swa_b_qkv, swa_sinks, swa_w_out,
              swa_b_out, ffn_w_gu, ffn_w_down):
    for layer in range(DEPTH):
        kind = layer % N_MIXERS
        j = layer // N_MIXERS
        h = rms_norm(x, mix_norm[layer])
        if kind == 0:
            y = retention(h, positions, ret_w_in[j], ret_w_out[j])
        elif kind == 1:
            y = rglru_block(h, lru_w_in[j], lru_conv_w[j], lru_conv_b[j], lru_w_r[j], lru_b_r[j],
                            lru_w_i[j], lru_b_i[j], lru_lambda[j], lru_w_out[j])
        else:
            y = sliding_window_sink_attention(h, positions, swa_w_qkv[j], swa_b_qkv[j],
                                              swa_sinks[j], swa_w_out[j], swa_b_out[j])
        x = x + y
        x = x + swiglu_ffn(rms_norm(x, ffn_norm[layer]), ffn_w_gu[layer], ffn_w_down[layer])
    return rms_norm(x, final_norm)


_drawn_inputs = setup_inputs


def setup_inputs(seed=0):
    import zlib

    import numpy as np

    out = dict(_drawn_inputs(seed))
    spreads = {}
    factors = {'ffn_norm': 3.118,
     'final_norm': 8.268,
     'lru_b_r': 37.222,
     'lru_b_i': 24.046,
     'lru_conv_b': 8.0}
    for name, (base, spread) in spreads.items():
        noise = np.random.default_rng([zlib.crc32(name.encode()), seed]).standard_normal(out[name].shape)
        drawn = base * np.exp(spread * noise) if base else spread * noise
        out[name] = jnp.asarray(drawn.astype(out[name].dtype))
    for name, factor in factors.items():
        out[name] = (out[name] * factor).astype(out[name].dtype)
    return out
```

```python
from contextlib import ExitStack

import concourse.bass as bass
from concourse import mybir
from concourse.alu_op_type import AluOpType as ALU

ACT = mybir.ActivationFunctionType
AX_X = mybir.AxisListType.X
F32 = mybir.dt.float32
F32R = mybir.dt.float32r
I32 = mybir.dt.int32

P = 128
D = 1024
S = 1024
KT = D // P
SB = S // P
BANK = 512
EPS = 1e-6
HEADS = 4
DK = D // HEADS
DV = 2 * D // HEADS
LRU = 1536
BLOCK_W = LRU // 8
GT = 3
GROUPS = LRU // (GT * P)
FFN = 2816
CT = 2
CHUNKS = FFN // (CT * P)
RING = 3

SCORES = ([(c, P * c, BANK - P * c) for c in range(4)]
          + [(c, q, 256) for c in range(4) for q in (512, 768)]
          + [(c, P * c, S - P * c) for c in range(4, 8)])
SCORE_AT = [sum(n for _, _, n in SCORES[:i]) for i in range(len(SCORES))]
SCORE_COLS = sum(n for _, _, n in SCORES)
MEETS = [(0, 1), (0, 1, 2), (1, 2)]

J_QK, J_S, J_G, J_V, J_O, J_T, J_W = 0, 8, 24, 32, 40, 48, 56
HEAD_JOBS = 72
CHUNK_JOBS = 24
NORM_JOBS = 16
JB_NORM = [0]
JB_RET = NORM_JOBS
JB_NORM.append(JB_RET + HEADS * HEAD_JOBS)
JB_FFN = [JB_NORM[1] + NORM_JOBS]
JB_NORM.append(JB_FFN[0] + CHUNKS * CHUNK_JOBS)
JB_LRU = JB_NORM[2] + NORM_JOBS
L_FIRST, L_TURN, L_LAST = 24, 40, 16
JB_NORM.append(JB_LRU + L_FIRST + (GROUPS - 1) * L_TURN + L_LAST)
JB_FFN.append(JB_NORM[3] + NORM_JOBS)
JOBS = JB_FFN[1] + CHUNKS * CHUNK_JOBS

HEAD_UNITS, CHUNK_UNITS = 32, 12
UB_FFN = [HEADS * HEAD_UNITS]
UB_LRU = UB_FFN[0] + CHUNKS * CHUNK_UNITS
UB_FFN.append(UB_LRU + GROUPS * 18)
UNITS = UB_FFN[1] + CHUNKS * CHUNK_UNITS

C_MIX, C_FFN, C_CONV, C_CONVB, C_BR, C_BI, C_LAM = 0, 16, 32, 80, 92, 104, 116


class Tally:

    def __init__(self, sem):
        self.sem, self.base, self.n, self.turn, self.per = sem, 0, 0, None, 0

    def loop(self, turn, per):
        self.turn, self.per, self.start = turn, per, self.n

    def end(self, turns):
        assert self.n - self.start == self.per, (self.n - self.start, self.per)
        self.n = self.start + self.per * turns
        self.turn = None

    def up(self, ins):
        self.n += 1
        ins.then_inc(self.sem, 1)
        return ins

    def now(self):
        return self.n if self.turn is None else self.turn * self.per + self.n


def build(nc, x, positions, mix_norm, ffn_norm, final_norm, ret_w_in, ret_w_out, lru_w_in, lru_conv_w,
          lru_conv_b, lru_w_r, lru_b_r, lru_w_i, lru_b_i, lru_lambda, lru_w_out, ffn_w_gu, ffn_w_down,
          inv_freq, decay, out):
    ctx = ExitStack()
    with ctx:
        def sb(name, cols, dt=F32, stack=ctx):
            return stack.enter_context(nc.sbuf_tensor(name, [P, cols], dt))

        def sem(name):
            return ctx.enter_context(nc.semaphore(name))

        X = sb("residual", SB * D)
        h_hi, h_lo = sb("h_hi", KT * S, F32R), sb("h_lo", KT * S, F32R)
        raw = sb("w_raw", RING * 512)
        w_hi, w_lo = sb("w_hi", RING * 512, F32R), sb("w_lo", RING * 512, F32R)
        T = sb("tmp", 3 * 512)
        R3 = sb("gate_buf", 8 * 512)
        ident = sb("ident", P)
        cols = sb("cols", P)
        gc_conv, gc_gate = sb("gc_conv", 24), sb("gc_gate", 24)
        ssq, rstd, invf, small = sb("ssq", 8), sb("rstd", 8), sb("invf", 1), sb("small", 72)
        with ExitStack() as one:
            xn = sb("xn", SB * D, F32, one)
        a_hi, a_lo = sb("a_hi", 4096, F32R), sb("a_lo", 4096, F32R)
        with ExitStack() as one:
            wri_hi, wri_lo = sb("wri_hi", 2304, F32R, one), sb("wri_lo", 2304, F32R, one)
            uc, wri_raw = sb("uc", 3072, F32, one), sb("wri_raw", 1152, F32, one)
        with ExitStack() as one:
            scr = sb("scratch", 9216, F32, one)
        with ExitStack() as one:
            pos = sb("pos", 1024, I32, one)
            turns_i = sb("turns_i", 1024, I32, one)
        b_hi, b_lo = sb("b_hi", SCORE_COLS, F32R), sb("b_lo", SCORE_COLS, F32R)
        assert SCORE_COLS == 4608
        ps = ctx.enter_context(nc.psum_tensor("ps", [P, 8 * BANK], F32))
        rope_dram = nc.dram_tensor("rope_tables", (2, P, S), F32, kind="Internal").ap()

        def bank(e, a=0, n=BANK):
            return ps[:, (e % 8) * BANK + a:(e % 8) * BANK + a + n]

        def t(i):
            return T[:, i * 512:(i + 1) * 512]

        def r3(i, n=1):
            return R3[:, i * 512:(i + n) * 512]

        x_in = [sem(f"x_in{i}") for i in range(SB)]
        vec_in, pos_in, fn_in = sem("vec_in"), sem("pos_in"), sem("fn_in")
        raw_in = [sem(f"raw_in{i}") for i in range(RING)]
        w_rounded, w_ready, w_begun = sem("w_rounded"), sem("w_ready"), sem("w_begun")
        ident_ready, vec_T, cols_ready = sem("ident_ready"), sem("vec_T"), sem("cols_ready")
        psum_full, psum_free = sem("psum_full"), sem("psum_free")
        dve_step, act_step = sem("dve_step"), sem("act_step")
        n_sq, n_var, n_root, xn_ready, h_rounded = (
            sem("n_sq"), sem("n_var"), sem("n_root"), sem("xn_ready"), sem("h_rounded"))
        table_arg, table_out, rope_saved = sem("table_arg"), sem("table_out"), sem("rope_saved")
        rope_in, decay_in = sem("rope_in"), sem("decay_in")
        rope_out, qk_rounded, qk_ready = sem("rope_out"), sem("qk_rounded"), sem("qk_ready")
        s_rounded, s_ready = sem("s_rounded"), sem("s_ready")
        g_sig = sem("g_sig")
        v_rounded = sem("v_rounded")
        o_sq, o_var, o_root, o_ready = sem("o_sq"), sem("o_var"), sem("o_root"), sem("o_ready")
        ot_rounded = sem("ot_rounded")
        f_sig, f_rounded, f_ready = sem("f_sig"), sem("f_rounded"), sem("f_ready")
        lam_e, lam_sp = sem("lam_e"), sem("lam_sp")
        wri_in, wri_zero, wri_round, wri_ready = (
            sem("wri_in"), sem("wri_zero"), sem("wri_round"), sem("wri_ready"))
        u_rounded, u_ready = sem("u_rounded"), sem("u_ready")
        gelu_done, gc_ready = sem("gelu_done"), sem("gc_ready")
        r_sig, i_sig, r_tanh, t_root = sem("r_sig"), sem("i_sig"), sem("r_tanh"), sem("t_root")
        l_scan, y_out, y_rounded, y_ready = (
            sem("l_scan"), sem("y_out"), sem("y_rounded"), sem("y_ready"))
        out_ready, out_done = sem("out_ready"), sem("out_done")
        block = ctx.enter_context(nc.Block())

        @block.sync
        def _(sp):
            vec = scr[:, 8 * 1024:8 * 1024 + P]
            for at, n, src in ((C_MIX, 16, mix_norm.rearrange("l (k p) -> (l k) p", p=P)),
                               (C_FFN, 16, ffn_norm.rearrange("l (k p) -> (l k) p", p=P)),
                               (C_CONV, 48, lru_conv_w[0].rearrange("j (k p) -> (j k) p", p=P)),
                               (C_CONVB, 12, lru_conv_b[0].rearrange("(k p) -> k p", p=P)),
                               (C_BR, 12, lru_b_r[0].rearrange("b c -> (b c)").rearrange("(k p) -> k p", p=P)),
                               (C_BI, 12, lru_b_i[0].rearrange("b c -> (b c)").rearrange("(k p) -> k p", p=P)),
                               (C_LAM, 12, lru_lambda[0].rearrange("(k p) -> k p", p=P))):
                sp.dma_start(vec[at:at + n, :], src).then_inc(vec_in, 16)
            sp.dma_start(pos[:], positions.to_broadcast([P, S])).then_inc(pos_in, 16)
            sp.dma_start(invf[:], inv_freq).then_inc(pos_in, 16)
            for s in range(SB):
                sp.dma_start(X[:, s * D:(s + 1) * D], x[0, s * P:(s + 1) * P, :]).then_inc(x_in[s], 16)

            def load(slot, src, ready):
                if ready is not None:
                    sp.wait_ge(w_ready, ready)
                dst = raw[:, slot * 512:(slot + 1) * 512]
                if len(src.shape) == 3:
                    dst = dst.rearrange("p (k n) -> p k n", k=4)
                sp.dma_start(dst, src).then_inc(raw_in[slot], 16)

            def rows(w, kh, col):
                return w[kh * 512:(kh + 1) * 512, bass.ds(col, P)].rearrange("(k p) n -> p k n", p=P)

            def last(u, j, restart):
                return u - 1 if restart and j < 2 else u - 2

            def head(h, first):
                for j in range(HEAD_UNITS):
                    if j < 8:
                        tile, kh = j // 2, j % 2
                        src = rows(ret_w_in[0], kh, (tile // 2) * D + h * DK + (tile % 2) * P)
                    elif j < 24:
                        k = (j - 8) % 8
                        off = (2 * D + HEADS * DV) if j < 16 else 2 * D
                        src = ret_w_in[0][k * P:(k + 1) * P, bass.ds(off + h * DV, DV)]
                    else:
                        nh, k = (j - 24) // 4, (j - 24) % 4
                        src = ret_w_out[0][bass.ds(h * DV + k * P, P), nh * 512:(nh + 1) * 512]
                    load(j % RING, src, None if first and j < RING else
                         last(h * HEAD_UNITS + j, j, not first))
            head(0, True)
            with sp.Fori(1, HEADS) as h:
                head(h, False)

            def ffn(layer):
                def chunk(c, restart):
                    for j in range(CHUNK_UNITS):
                        if j < 8:
                            tile, up, kh = j // 4, (j // 2) % 2, j % 2
                            src = rows(ffn_w_gu[layer], kh, up * FFN + c * (CT * P) + tile * P)
                        else:
                            nh, k = (j - 8) // 2, j % 2
                            src = ffn_w_down[layer][bass.ds(c * (CT * P) + k * P, P), nh * 512:(nh + 1) * 512]
                        load(j % RING, src, last(UB_FFN[layer] + c * CHUNK_UNITS + j, j, restart))
                chunk(0, layer == 0)
                with sp.Fori(1, CHUNKS) as c:
                    chunk(c, False)

            ffn(0)

            def gates(g, w, n, behind=None):
                sp.wait_ge(wri_ready, n)
                sp.wait_ge(wri_zero, 1)
                a = w[0][bass.ds(2 * g, 1)].rearrange("a c d -> (a c) d")
                b = w[0][bass.ds(2 * g + 1, 1)].rearrange("a c d -> (a c) d")
                r = wri_raw
                pieces = ((r[:, 0:192], a[0:128, :]), (r[0:64, 384:576], a[128:192, :]),
                          (r[64:128, 576:768], b[0:64, :]), (r[:, 960:1152], b[64:192, :]))
                for dst, src in pieces:
                    if behind is not None and dst is pieces[-1][0]:
                        sp.wait_ge(w_ready, behind)
                    sp.dma_start(dst, src).then_inc(wri_in, 16)

            def into(g, gate, u0, waited=False):
                for j in range(6):
                    tile, kh = j // 2, j % 2
                    src = rows(lru_w_in[0], kh, (0 if gate else LRU) + g * (GT * P) + tile * P)
                    load(j % RING, src, None if waited and j == 0 else last(u0 + j, j, False))

            def outof(g, u0):
                for j in range(6):
                    nh, k = j // 3, j % 3
                    src = lru_w_out[0][bass.ds(g * (GT * P) + k * P, P), nh * 512:(nh + 1) * 512]
                    load(j % RING, src, last(u0 + j, j, False))

            into(0, False, UB_LRU)
            gates(0, lru_w_r, 0)
            into(0, True, UB_LRU + 6)
            gates(0, lru_w_i, 1)
            with sp.Fori(1, GROUPS) as g:
                u0 = UB_LRU + g * 18 - 6
                into(g, False, u0)
                gates(g, lru_w_r, 2 * g, last(u0 + 6, 0, False))
                into(g, True, u0 + 6, waited=True)
                gates(g, lru_w_i, 2 * g + 1)
                outof(g - 1, u0 + 12)
            outof(GROUPS - 1, UB_LRU + GROUPS * 18 - 6)
            ffn(1)
            sp.wait_ge(psum_free, JB_NORM[3])
            sp.dma_start(scr[:, 0:D], final_norm.rearrange("(a n) -> a n", a=1).to_broadcast([P, D]))\
              .then_inc(fn_in, 16)
            for s in range(SB):
                sp.wait_ge(out_ready, s + 1)
                sp.dma_start(out[0, s * P:(s + 1) * P, :], xn[:, s * D:(s + 1) * D]).then_inc(out_done, 16)
            sp.wait_ge(out_done, 16 * SB)

        @block.gpsimd
        def _(pool):
            nc.gpsimd.memset(ident[:], 0.0).then_inc(ident_ready, 1)
            pool.wait_ge(ident_ready, 1)
            nc.gpsimd.affine_select(out=ident[:], in_=ident[:], compare_op=ALU.not_equal, fill=1.0, base=0,
                                    pattern=[[-1, P]], channel_multiplier=1).then_inc(ident_ready, 1)

            def touch(col):
                nc.gpsimd.tensor_tensor(small[:, 62:63], col, col, ALU.subtract)

            def split(slot, loads, u, used):
                cut = slice(slot * 512, (slot + 1) * 512)
                pool.wait_ge(raw_in[slot], loads)
                if used is not None:
                    pool.wait_ge(w_begun, used)
                touch(raw[:, slot * 512:slot * 512 + 1])
                nc.gpsimd.tensor_copy(w_hi[:, cut], raw[:, cut]).then_inc(w_rounded, 1)
                pool.wait_ge(w_rounded, u + 1)
                nc.gpsimd.tensor_tensor(w_lo[:, cut], raw[:, cut], w_hi[:, cut].bitcast(F32),
                                        ALU.subtract).then_inc(w_ready, 1)

            def head(h, first):
                for j in range(HEAD_UNITS):
                    u, slot = h * HEAD_UNITS + j, j % RING
                    used = None if first and j < RING else u if j < 2 else u - 1
                    split(slot, 16 * (h * (11 if slot < 2 else 10) + j // RING + 1), u, used)
            head(0, True)
            with pool.Fori(1, HEADS) as h:
                head(h, False)
            landed = [HEADS * (11 if slot < 2 else 10) for slot in range(RING)]

            def units(n, u0, before, restart=False):
                for j in range(n):
                    split(j % RING, 16 * (before[j % RING] + j // RING + 1), u0 + j,
                          u0 + j - (0 if restart and j < 2 else 1))

            def ffn(layer, landed):
                def chunk(c, restart):
                    units(CHUNK_UNITS, UB_FFN[layer] + c * CHUNK_UNITS, [c * 4 + n for n in landed], restart)
                chunk(0, layer == 0)
                with pool.Fori(1, CHUNKS) as c:
                    chunk(c, False)

            ffn(0, landed)
            landed = [n + 4 * CHUNKS for n in landed]
            pool.wait_ge(psum_full, JB_LRU)
            nc.gpsimd.memset(wri_raw[:], 0.0).then_inc(wri_zero, 1)

            def gates(g, n, at):
                pool.wait_ge(wri_in, 64 * (n + 1))
                touch(wri_raw[:, 0:1])
                cut = slice(at * 1152, (at + 1) * 1152)
                nc.gpsimd.tensor_copy(wri_hi[:, cut], wri_raw[:]).then_inc(wri_round, 1)
                pool.wait_ge(wri_round, n + 1)
                nc.gpsimd.tensor_tensor(wri_lo[:, cut], wri_raw[:], wri_hi[:, cut].bitcast(F32),
                                        ALU.subtract).then_inc(wri_ready, 1)

            units(6, UB_LRU, landed)
            gates(0, 0, 0)
            units(6, UB_LRU + 6, [n + 2 for n in landed])
            gates(0, 1, 1)
            with pool.Fori(1, GROUPS) as g:
                u0 = UB_LRU + g * 18 - 6
                now = [n + g * 6 - 2 for n in landed]
                units(6, u0, now)
                pool.wait_ge(psum_full, JB_LRU + L_FIRST + (g - 1) * L_TURN + 1)
                gates(g, 2 * g, 0)
                units(6, u0 + 6, [n + 2 for n in now])
                gates(g, 2 * g + 1, 1)
                units(6, u0 + 12, [n + 4 for n in now])
            units(6, UB_LRU + GROUPS * 18 - 6, [n + GROUPS * 6 - 2 for n in landed])
            ffn(1, [n + GROUPS * 6 for n in landed])

        @block.tensor
        def _(pe):
            def free(e):
                pe.wait_ge(psum_free, e - 7)

            def three(o, l_hi, l_lo, r_hi, r_lo, start, stop, begins=False):
                m = nc.tensor.matmul(o, l_hi, r_hi, start=start, stop=False)
                if begins:
                    m.then_inc(w_begun, 1)
                nc.tensor.matmul(o, l_hi, r_lo, start=False, stop=False)
                return nc.tensor.matmul(o, l_lo, r_hi, start=False, stop=stop)

            def rows_unit(j, u, kh, banks):
                pe.wait_ge(w_ready, u + 1)
                for kk in range(4):
                    w = slice((j % RING) * 512 + kk * P, (j % RING) * 512 + (kk + 1) * P)
                    for hf in range(2):
                        r = slice((kh * 4 + kk) * S + hf * 512, (kh * 4 + kk) * S + (hf + 1) * 512)
                        m = three(bank(banks[hf]), w_hi[:, w], w_lo[:, w], h_hi[:, r], h_lo[:, r],
                                  kh == 0 and kk == 0, kh == 1 and kk == 3, kk == 0 and hf == 0)
                        if kh == 1 and kk == 3:
                            m.then_inc(psum_full, 1)

            def cols_unit(j, u, k, nk, l_hi, l_lo, at, e0, base, ready=None):
                pe.wait_ge(w_ready, u + 1)
                w = slice((j % RING) * 512, (j % RING + 1) * 512)
                for s in range(SB):
                    if k == 0:
                        free(base + e0 + s)
                    if ready is not None:
                        pe.wait_ge(ready[0], ready[1](s))
                    c = at + s * P
                    m = three(bank(e0 + s), l_hi[:, c:c + P], l_lo[:, c:c + P], w_hi[:, w], w_lo[:, w],
                              k == 0, k == nk - 1, s == 0)
                    if k == nk - 1:
                        m.then_inc(psum_full, 1)

            def tile_rows(j, u, e0, base, banks, wait):
                free(base + wait)
                rows_unit(j, u, 0, banks)
                rows_unit(j + 1, u + 1, 1, banks)

            def norm(n, count):
                for hf in range(2):
                    for k in range(KT):
                        e = JB_NORM[n] + hf * 8 + k
                        if e >= 8:
                            free(e)
                        for s in range(4):
                            if k == 0:
                                pe.wait_ge(xn_ready, 8 * n + hf * 4 + s + 1)
                            c = (hf * 4 + s) * D + k * P
                            m = nc.tensor.transpose(bank(e, s * P, P), xn[:, c:c + P], ident[:])
                        m.then_inc(psum_full, 1)
                pe.wait_ge(psum_free, JB_NORM[n] + NORM_JOBS)

            pe.wait_ge(vec_in, 16 * 7)
            pe.wait_ge(ident_ready, 2)
            nc.tensor.transpose(ps[:, 7 * BANK:7 * BANK + P], scr[:, 8 * 1024:8 * 1024 + P],
                                ident[:]).then_inc(vec_T, 1)
            pe.wait_ge(cols_ready, 1)
            norm(0, 0)

            with pe.Fori(0, HEADS) as h:
                base, ub = JB_RET + h * HEAD_JOBS, h * HEAD_UNITS
                for tile in range(4):
                    b = 4 * (tile // 2) + tile % 2
                    tile_rows(2 * tile, ub + 2 * tile, J_QK, base, (b, b + 2), b + 2)
                for i, (c, q, n) in enumerate(SCORES):
                    if i == 0:
                        pe.wait_ge(qk_ready, h * 8 + 8)
                    free(base + J_S + i)
                    for d in range(2):
                        kc, qc = (2 + d) * S + c * P, d * S + q
                        m = three(bank(J_S + i, 0, n), a_hi[:, kc:kc + P], a_lo[:, kc:kc + P],
                                  a_hi[:, qc:qc + n], a_lo[:, qc:qc + n], d == 0, d == 1)
                    m.then_inc(psum_full, 1)
                for k in range(KT):
                    cols_unit(8 + k, ub + 8 + k, k, KT, h_hi, h_lo, k * S, J_G, base)
                for k in range(KT):
                    cols_unit(16 + k, ub + 16 + k, k, KT, h_hi, h_lo, k * S, J_V, base)
                pe.wait_ge(s_ready, h * 16 + 16)
                for s in range(SB):
                    free(base + J_O + s)
                    pe.wait_ge(psum_free, base + J_V + s + 1)
                    for c in range(s + 1):
                        i = next(i for i, (cc, q, n) in enumerate(SCORES) if cc == c and q <= s * P < q + n)
                        a = SCORE_AT[i] + s * P - SCORES[i][1]
                        m = three(bank(J_O + s), b_hi[:, a:a + P], b_lo[:, a:a + P],
                                  a_hi[:, c * 512:(c + 1) * 512], a_lo[:, c * 512:(c + 1) * 512],
                                  c == 0, c == s)
                    m.then_inc(psum_full, 1)
                for s in range(SB):
                    free(base + J_T + s)
                    pe.wait_ge(o_ready, h * 8 + s + 1)
                    for d in range(4):
                        m = nc.tensor.transpose(bank(J_T + s, d * P, P),
                                                R3[:, s * 512 + d * P:s * 512 + (d + 1) * P], ident[:])
                    m.then_inc(psum_full, 1)
                for nh in range(2):
                    for k in range(4):
                        j = 24 + nh * 4 + k
                        cols_unit(j, ub + j, k, 4, b_hi, b_lo, k * S, J_W + nh * 8, base,
                                  (psum_free, lambda s: base + J_T + s + 1) if nh == 0 and k == 0 else None)

            def ffn(layer):
                with pe.Fori(0, CHUNKS) as c:
                    base, ub = JB_FFN[layer] + c * CHUNK_JOBS, UB_FFN[layer] + c * CHUNK_UNITS
                    for i in range(4):
                        b = 4 * (i // 2) + i % 2
                        tile_rows(2 * i, ub + 2 * i, 0, base, (b, b + 2), b + 2)
                    for nh in range(2):
                        for k in range(CT):
                            if nh == 0:
                                pe.wait_ge(f_ready, (layer * CHUNKS + c) * 4 + 2 * k + 2)
                            j = 8 + nh * 2 + k
                            cols_unit(j, ub + j, k, CT, a_hi, a_lo, k * S, 8 + nh * 8, base)

            norm(1, 0)
            ffn(0)
            norm(2, 0)

            def lru_into(u0, base, e0):
                for tile in range(GT):
                    e = e0 + 2 * tile
                    tile_rows(2 * tile, u0 + 2 * tile, e, base, (e, e + 1), e + 1)

            def lru_gates(g, base, e0):
                pe.wait_ge(wri_ready, 2 * g + 2)
                pe.wait_ge(u_ready, 3 * g + 3)
                for hf in range(2):
                    for tile in range(GT):
                        for m_i in range(2):
                            e = e0 + (hf * GT + tile) * 2 + m_i
                            free(base + e)
                            for kt in MEETS[tile]:
                                w = slice(m_i * 1152 + kt * 384 + tile * P, m_i * 1152 + kt * 384 + (tile + 1) * P)
                                r = slice(kt * S + hf * 512, kt * S + (hf + 1) * 512)
                                m = three(bank(e), wri_hi[:, w], wri_lo[:, w], a_hi[:, r], a_lo[:, r],
                                          kt == MEETS[tile][0], kt == MEETS[tile][-1])
                            m.then_inc(psum_full, 1)

            def lru_outof(g, u0, base, e0):
                for nh in range(2):
                    for k in range(GT):
                        j = nh * 3 + k
                        if nh == 0:
                            pe.wait_ge(y_ready, g * 6 + k + 4)
                        cols_unit(j, u0 + j, k, GT, a_hi, a_lo, k * S, e0 + nh * 8, base)

            lru_into(UB_LRU, JB_LRU, 0)
            lru_into(UB_LRU + 6, JB_LRU, 6)
            lru_gates(0, JB_LRU, 12)
            with pe.Fori(1, GROUPS) as g:
                base, u0 = JB_LRU + L_FIRST + (g - 1) * L_TURN, UB_LRU + g * 18 - 6
                lru_into(u0, base, 0)
                lru_into(u0 + 6, base, 6)
                lru_outof(g - 1, u0 + 12, base, 12)
                lru_gates(g, base, 28)
            lru_outof(GROUPS - 1, UB_LRU + GROUPS * 18 - 6, JB_LRU + L_FIRST + (GROUPS - 1) * L_TURN, 0)
            norm(3, 0)
            ffn(1)

        @block.scalar
        def _(act):
            def full(e):
                act.wait_ge(psum_full, e + 1)

            def square_rows(s, n):
                nc.scalar.activation(xn[:, s * D:(s + 1) * D], X[:, s * D:(s + 1) * D], ACT.Square,
                                     accum_out=ssq[:, s:s + 1]).then_inc(n_sq, 1)

            def norm(n):
                if n:
                    act.wait_ge(psum_free, JB_NORM[n])
                for hf in range(2):
                    for s in range(hf * 4, hf * 4 + 4):
                        if n == 0:
                            act.wait_ge(x_in[s], 16)
                        square_rows(s, n)
                    act.wait_ge(n_var, 2 * n + hf + 1)
                    nc.scalar.activation(rstd[:, hf * 4:hf * 4 + 4], ssq[:, hf * 4:hf * 4 + 4],
                                         ACT.Sqrt).then_inc(n_root, 1)
                if n == 0:
                    act.wait_ge(cols_ready, 1)
                for hf in range(2):
                    for k in range(KT):
                        e = JB_NORM[n] + hf * 8 + k
                        full(e)
                        g = (C_MIX + (n // 2) * 8 if n % 2 == 0 else C_FFN + (n // 2) * 8) + k
                        nc.scalar.activation(h_hi[:, k * S + hf * 512:k * S + (hf + 1) * 512], bank(e),
                                             ACT.Copy, scale=cols[:, g:g + 1]).then_inc(h_rounded, 1)

            norm(0)
            for i in range(2):
                act.wait_ge(table_arg, i + 1)
                nc.scalar.activation(scr[:, (4 + i) * S:(5 + i) * S], scr[:, (2 + i) * S:(3 + i) * S],
                                     ACT.Sin).then_inc(table_out, 1)
                act.wait_ge(table_out, i + 1)
                act.dma_start(rope_dram[i], scr[:, (4 + i) * S:(5 + i) * S]).then_inc(rope_saved, 16)
            act.wait_ge(lam_e, 1)
            nc.scalar.activation(small[:, 12:24], small[:, 0:12], ACT.Exp).then_inc(lam_sp, 1)
            act.wait_ge(rope_saved, 32)

            with act.Fori(0, HEADS) as h:
                base = JB_RET + h * HEAD_JOBS
                act.wait_ge(psum_full, base)
                act.dma_start(R3[:, 0:S], rope_dram[1]).then_inc(rope_in, 16)
                act.dma_start(R3[:, S:2 * S], rope_dram[0]).then_inc(rope_in, 16)
                act.dma_start(R3[:, 2 * S:3 * S], decay[bass.ds(h, 1)].rearrange("a p n -> (a p) n")).then_inc(decay_in, 16)
                for i in range(8):
                    pair, hf, d = i // 4, (i // 2) % 2, i % 2
                    act.wait_ge(rope_out, h * 8 + i + 1)
                    c = (2 * pair + d) * S + hf * 512
                    nc.scalar.activation(a_hi[:, c:c + 512], t(2) if d == 0 else r3(6), ACT.Copy)\
                        .then_inc(qk_rounded, 1)
                for i, (c, q, n) in enumerate(SCORES):
                    act.wait_ge(psum_free, base + J_S + i + 1)
                    nc.scalar.activation(b_hi[:, SCORE_AT[i]:SCORE_AT[i] + n], T[:, (i % 3) * 512:(i % 3) * 512 + n],
                                         ACT.Copy).then_inc(s_rounded, 1)
                for s in range(SB):
                    full(base + J_G + s)
                    if s == 0:
                        act.wait_ge(s_ready, h * 16 + 16)
                    if s >= 3:
                        act.wait_ge(psum_free, base + J_G + s - 2)
                    nc.scalar.activation(t(s % 3), bank(J_G + s), ACT.Sigmoid).then_inc(g_sig, 1)
                for s in range(SB):
                    full(base + J_V + s)
                    nc.scalar.activation(a_hi[:, s * 512:(s + 1) * 512], bank(J_V + s), ACT.Copy)\
                        .then_inc(v_rounded, 1)
                act.wait_ge(psum_free, base + J_V)
                for s in range(SB):
                    full(base + J_O + s)
                    if s >= 3:
                        act.wait_ge(o_sq, h * 8 + s - 2)
                    nc.scalar.activation(t(s % 3), bank(J_O + s), ACT.Square,
                                         accum_out=ssq[:, s:s + 1]).then_inc(o_sq, 1)
                act.wait_ge(o_var, h + 1)
                nc.scalar.activation(rstd[:], ssq[:], ACT.Sqrt).then_inc(o_root, 1)
                for s in range(SB):
                    full(base + J_T + s)
                    nc.scalar.activation(b_hi[:, 0:4096].rearrange("p (d n) -> p d n", d=4)[:, :, s * P:(s + 1) * P],
                                         bank(J_T + s).rearrange("p (d n) -> p d n", d=4), ACT.Copy)\
                        .then_inc(ot_rounded, 1)

            def ffn(layer):
                with act.Fori(0, CHUNKS) as c:
                    base, n = JB_FFN[layer] + c * CHUNK_JOBS, (layer * CHUNKS + c) * 4

                    def rounded(i):
                        act.wait_ge(psum_free, base + 2 * i + 2)
                        at = (i // 2) * S + (i % 2) * 512
                        nc.scalar.activation(a_hi[:, at:at + 512], r3(4 + i), ACT.Copy).then_inc(f_rounded, 1)

                    for tile in range(CT):
                        for hf in range(2):
                            i = tile * 2 + hf
                            act.wait_ge(psum_full, base + 4 * tile + hf + 1)
                            nc.scalar.activation(r3(i), bank(4 * tile + 2 * hf), ACT.Sigmoid).then_inc(f_sig, 1)
                        rounded(2 * tile)
                        rounded(2 * tile + 1)

            norm(1)
            ffn(0)
            norm(2)

            def gelu(g, base, e0):
                for tile in range(GT):
                    full(base + e0 + 2 * tile + 1)
                    act.wait_ge(y_ready, g * 6)
                    b = (e0 + 2 * tile) % 8 * BANK
                    nc.scalar.activation(R3[:, tile * S:(tile + 1) * S], ps[:, b:b + 2 * BANK],
                                         ACT.Gelu_apprx_tanh).then_inc(gelu_done, 1)

            def u_round(g, base):
                for tile in range(GT):
                    act.wait_ge(psum_free, base + 2 * tile + 2)
                    nc.scalar.activation(a_hi[:, tile * S:(tile + 1) * S], uc[:, tile * S:(tile + 1) * S],
                                         ACT.Copy).then_inc(u_rounded, 1)

            def gate_chain(g, base, e0):
                def y_round(i):
                    act.wait_ge(y_out, 6 * g + i + 1)
                    act.wait_ge(psum_full, base + e0 + (6 if i < GT else 12))
                    at = i % GT * S + i // GT * 512
                    nc.scalar.activation(a_hi[:, at:at + 512], t(2), ACT.Copy).then_inc(y_rounded, 1)

                act.wait_ge(gc_ready, g + 1)
                for i in range(6):
                    tile = i % GT
                    tr, ti = (t(0), t(1)) if i % 2 == 0 else (r3(6), r3(7))
                    if i >= 2:
                        act.wait_ge(l_scan, 6 * g + i - 1)
                    full(base + e0 + 2 * i)
                    nc.scalar.activation(tr, bank(e0 + 2 * i), ACT.Sigmoid,
                                         bias=gc_gate[:, 15 + tile:16 + tile]).then_inc(r_sig, 1)
                    full(base + e0 + 2 * i + 1)
                    nc.scalar.activation(ti, bank(e0 + 2 * i + 1), ACT.Sigmoid,
                                         bias=gc_gate[:, 18 + tile:19 + tile]).then_inc(i_sig, 1)
                    act.wait_ge(r_sig, 6 * g + i + 1)
                    nc.scalar.activation(tr, tr, ACT.Tanh, scale=gc_gate[:, 21 + tile:22 + tile])\
                        .then_inc(r_tanh, 1)
                    if i:
                        y_round(i - 1)
                    act.wait_ge(r_tanh, 6 * g + i + 1)
                    act.wait_ge(psum_free, base + e0 + 2 * i + 2)
                    nc.scalar.activation(ti, tr, ACT.Sqrt).then_inc(t_root, 1)
                y_round(5)

            gelu(0, JB_LRU, 6)
            u_round(0, JB_LRU)
            gate_chain(0, JB_LRU, 12)
            with act.Fori(1, GROUPS) as g:
                base = JB_LRU + L_FIRST + (g - 1) * L_TURN
                gelu(g, base, 6)
                act.wait_ge(psum_full, base + 28)
                u_round(g, base)
                gate_chain(g, base, 28)
            norm(3)
            ffn(1)
            act.wait_ge(psum_free, JOBS)
            for s in range(SB):
                square_rows(s, 4)
            act.wait_ge(n_var, 9)
            nc.scalar.activation(rstd[:], ssq[:], ACT.Sqrt).then_inc(n_root, 1)

        @block.vector
        def _(dve):
            step = Tally(dve_step)

            def link(ins):
                step.up(ins)
                dve.wait_ge(dve_step, step.now())

            def full(e):
                dve.wait_ge(psum_full, e + 1)

            TT, TS, STT = nc.vector.tensor_tensor, nc.vector.tensor_scalar, nc.vector.scalar_tensor_tensor

            def norm(n):
                for hf in range(2):
                    q = slice(hf * 4, hf * 4 + 4)
                    dve.wait_ge(n_sq, 8 * n + hf * 4 + 4)
                    TS(ssq[:, q], ssq[:, q], 1.0 / D, EPS, ALU.mult, ALU.add).then_inc(n_var, 1)
                    dve.wait_ge(n_root, 2 * n + hf + 1)
                    link(nc.vector.reciprocal(rstd[:, q], rstd[:, q]))
                    for s in range(hf * 4, hf * 4 + 4):
                        TS(xn[:, s * D:(s + 1) * D], X[:, s * D:(s + 1) * D], rstd[:, s:s + 1], None,
                           ALU.mult).then_inc(xn_ready, 1)
                for hf in range(2):
                    for k in range(KT):
                        e = JB_NORM[n] + hf * 8 + k
                        g = (C_MIX + (n // 2) * 8 if n % 2 == 0 else C_FFN + (n // 2) * 8) + k
                        c = slice(k * S + hf * 512, k * S + (hf + 1) * 512)
                        dve.wait_ge(h_rounded, 16 * n + hf * 8 + k + 1)
                        i = STT(h_lo[:, c], bank(e), cols[:, g:g + 1], h_hi[:, c].bitcast(F32),
                                ALU.mult, ALU.subtract)
                        i.then_inc(psum_free, 1)

            dve.wait_ge(vec_T, 1)
            nc.vector.tensor_copy(cols[:], ps[:, 7 * BANK:7 * BANK + P]).then_inc(cols_ready, 1)
            norm(0)

            dve.wait_ge(pos_in, 32)
            ang, tmp, rs, rc = (scr[:, i * S:(i + 1) * S] for i in (6, 7, 2, 3))
            link(nc.vector.tensor_copy(tmp, pos[:]))
            link(TS(ang, tmp, invf[:], None, ALU.mult))
            parts = (6.28125, 0.00193500518798828125, 3.01991598196e-07)
            for unit in (4096.0, 1.0):
                link(TS(tmp, ang, 1.0 / (6.283185307179586 * unit), None, ALU.mult))
                link(nc.vector.tensor_copy(turns_i[:], tmp))
                link(nc.vector.tensor_copy(tmp, turns_i[:]))
                for part in parts:
                    link(STT(ang, tmp, -part * unit, ang, ALU.mult, ALU.add))
            TS(rs, ang, 3.1415925, -3.1415925, ALU.min, ALU.max).then_inc(table_arg, 1)
            dve.wait_ge(table_arg, 1)
            link(STT(rc, rs, -1.0, rs, ALU.mult, ALU.max))
            TS(rc, rc, -1.0, 1.5707963267948966, ALU.mult, ALU.add).then_inc(table_arg, 1)
            lam = cols[:, C_LAM:C_LAM + 12]
            link(TS(small[:, 24:36], lam, -1.0, None, ALU.mult))
            TT(small[:, 0:12], lam, small[:, 24:36], ALU.min).then_inc(lam_e, 1)
            dve.wait_ge(lam_e, 1)
            link(TS(small[:, 24:36], small[:, 24:36], 0.0, None, ALU.max))
            dve.wait_ge(lam_sp, 1)
            z, zz, acc = small[:, 0:12], small[:, 36:48], small[:, 48:60]
            link(TS(z, small[:, 12:24], 2.0, None, ALU.add))
            link(nc.vector.reciprocal(z, z))
            link(TT(z, z, small[:, 12:24], ALU.mult))
            link(TT(zz, z, z, ALU.mult))
            link(TS(acc, zz, 1.0 / 17, 1.0 / 15, ALU.mult, ALU.add))
            for n in (13, 11, 9, 7, 5, 3, 1):
                link(TT(acc, acc, zz, ALU.mult))
                link(TS(acc, acc, 1.0 / n, None, ALU.add))
            link(TT(acc, acc, z, ALU.mult))
            link(STT(acc, acc, 2.0, small[:, 24:36], ALU.mult, ALU.add))
            link(TS(cols[:, C_LAM:C_LAM + 12], acc, 4.0, None, ALU.mult))

            def add(e, le, s, nh):
                c = slice(s * D + nh * 512, s * D + (nh + 1) * 512)
                full(e)
                TT(X[:, c], bank(le), X[:, c], ALU.add).then_inc(psum_free, 1)

            with dve.Fori(0, HEADS) as h:
                base = JB_RET + h * HEAD_JOBS
                step.loop(h, 1)
                dve.wait_ge(rope_in, h * 32 + 32)
                for pair in range(2):
                    dve.wait_ge(psum_full, base + 4 * pair + 4)
                    for hf in range(2):
                        b = 4 * pair + 2 * hf
                        cs, sn = R3[:, hf * 512:(hf + 1) * 512], R3[:, S + hf * 512:S + (hf + 1) * 512]
                        TT(t(0), bank(b), cs, ALU.mult)
                        TT(r3(6), bank(b + 1), cs, ALU.mult)
                        TT(r3(7), bank(b), sn, ALU.mult).then_inc(psum_free, 1)
                        i = TT(t(1), bank(b + 1), sn, ALU.mult)
                        i.then_inc(psum_free, 1)
                        dve.wait_ge(psum_free, base + 4 * pair + 2 * hf + 2)
                        TT(t(2), t(0), t(1), ALU.subtract).then_inc(rope_out, 1)
                        TT(r3(6), r3(6), r3(7), ALU.add).then_inc(rope_out, 1)
                        n = h * 8 + (pair * 2 + hf) * 2
                        for d, src in ((0, t(2)), (1, r3(6))):
                            c = slice((2 * pair + d) * S + hf * 512, (2 * pair + d) * S + (hf + 1) * 512)
                            dve.wait_ge(qk_rounded, n + d + 1)
                            i = TT(a_lo[:, c], src, a_hi[:, c].bitcast(F32), ALU.subtract)
                            i.then_inc(qk_ready, 1)
                        dve.wait_ge(qk_ready, n + 2)
                dve.wait_ge(decay_in, h * 16 + 16)
                for i in range(len(SCORES) + 1):
                    if i < len(SCORES):
                        c, q, n = SCORES[i]
                        if i >= 3:
                            dve.wait_ge(s_ready, h * 16 + i - 2)
                        full(base + J_S + i)
                        k = TT(T[:, (i % 3) * 512:(i % 3) * 512 + n], bank(J_S + i, 0, n),
                               R3[:, 2 * S + q - c * P:2 * S + q - c * P + n], ALU.mult)
                        k.then_inc(psum_free, 1)
                    if i:
                        n, a = SCORES[i - 1][2], SCORE_AT[i - 1]
                        dve.wait_ge(s_rounded, h * 16 + i)
                        TT(b_lo[:, a:a + n], T[:, ((i - 1) % 3) * 512:((i - 1) % 3) * 512 + n],
                           b_hi[:, a:a + n].bitcast(F32), ALU.subtract).then_inc(s_ready, 1)
                for s in range(SB):
                    dve.wait_ge(g_sig, h * 8 + s + 1)
                    i = TT(r3(s), bank(J_G + s), t(s % 3), ALU.mult)
                    i.then_inc(psum_free, 1)
                for s in range(SB):
                    dve.wait_ge(v_rounded, h * 8 + s + 1)
                    c = slice(s * 512, (s + 1) * 512)
                    i = TT(a_lo[:, c], bank(J_V + s), a_hi[:, c].bitcast(F32), ALU.subtract)
                    i.then_inc(psum_free, 1)
                for s in range(SB):
                    dve.wait_ge(o_sq, h * 8 + s + 1)
                    i = TT(r3(s), bank(J_O + s), r3(s), ALU.mult)
                    i.then_inc(psum_free, 1)
                TS(ssq[:], ssq[:], 1.0 / DV, EPS, ALU.mult, ALU.add).then_inc(o_var, 1)
                dve.wait_ge(psum_free, base + J_T)
                dve.wait_ge(o_root, h + 1)
                link(nc.vector.reciprocal(rstd[:], rstd[:]))
                for s in range(SB):
                    TS(r3(s), r3(s), rstd[:, s:s + 1], None, ALU.mult).then_inc(o_ready, 1)
                for s in range(SB):
                    dve.wait_ge(ot_rounded, h * 8 + s + 1)
                    cut = (slice(None), slice(None), slice(s * P, (s + 1) * P))
                    i = TT(b_lo[:, 0:4096].rearrange("p (d n) -> p d n", d=4)[cut],
                           bank(J_T + s).rearrange("p (d n) -> p d n", d=4),
                           b_hi[:, 0:4096].rearrange("p (d n) -> p d n", d=4)[cut].bitcast(F32), ALU.subtract)
                    i.then_inc(psum_free, 1)
                for nh in range(2):
                    for s in range(SB):
                        add(base + J_W + nh * 8 + s, J_W + nh * 8 + s, s, nh)
            step.end(HEADS)

            def ffn(layer):
                with dve.Fori(0, CHUNKS) as c:
                    base, n = JB_FFN[layer] + c * CHUNK_JOBS, (layer * CHUNKS + c) * 4
                    for tile in range(CT):
                        for hf in range(2):
                            i = tile * 2 + hf
                            dve.wait_ge(f_sig, n + i + 1)
                            k = TT(r3(4 + i), bank(4 * tile + 2 * hf), r3(i), ALU.mult)
                            k.then_inc(psum_free, 1)
                            dve.wait_ge(psum_free, base + 4 * tile + 2 * hf + 1)
                            full(base + 4 * tile + 2 + hf)
                            k = TT(r3(4 + i), r3(4 + i), bank(4 * tile + 2 * hf + 1), ALU.mult)
                            k.then_inc(psum_free, 1)
                        for i in (2 * tile, 2 * tile + 1):
                            dve.wait_ge(f_rounded, n + i + 1)
                            at = slice((i // 2) * S + (i % 2) * 512, (i // 2) * S + (i % 2) * 512 + 512)
                            TT(a_lo[:, at], r3(4 + i), a_hi[:, at].bitcast(F32), ALU.subtract)\
                                .then_inc(f_ready, 1)
                    for nh in range(2):
                        for s in range(SB):
                            add(base + 8 + nh * 8 + s, 8 + nh * 8 + s, s, nh)

            norm(1)
            ffn(0)
            norm(2)

            group_cols = cols[:, C_CONV:C_CONV + 96].rearrange("p (q c) -> p q c", q=8)

            def take(dst, g):
                return nc.vector.tensor_copy(dst[:].rearrange("p (q c) -> p q c", q=8),
                                             group_cols[:, :, bass.ds(GT * g, GT)])

            def conv(g, base, e0):
                link(take(gc_conv, g))
                for tile in range(GT):
                    full(base + e0 + 2 * tile + 1)
                    b = (e0 + 2 * tile) % 8 * BANK
                    u = uc[:, tile * S:(tile + 1) * S]

                    def w(j):
                        return gc_conv[:, 3 * j + tile:3 * j + tile + 1]

                    link(TS(u, ps[:, b:b + S], w(3), w(4), ALU.mult, ALU.add))
                    for back in (1, 2, 3):
                        i = STT(u[:, back:], ps[:, b:b + S - back], w(3 - back), u[:, back:], ALU.mult, ALU.add)
                        if back < 3:
                            link(i)
                    i.then_inc(psum_free, 2)

            def gelu_seen(g, e0):
                for tile in range(GT):
                    dve.wait_ge(gelu_done, 3 * g + tile + 1)
                    nc.vector.memset(small[:, 64 + tile:65 + tile], 0.0).then_inc(psum_free, 2)

            def u_split(g):
                for tile in range(GT):
                    c = slice(tile * S, (tile + 1) * S)
                    dve.wait_ge(u_rounded, 3 * g + tile + 1)
                    TT(a_lo[:, c], uc[:, c], a_hi[:, c].bitcast(F32), ALU.subtract).then_inc(u_ready, 1)

            def gate_chain(g):
                take(gc_gate, g).then_inc(gc_ready, 1)
                for i in range(6):
                    tr, ti = (t(0), t(1)) if i % 2 == 0 else (r3(6), r3(7))
                    tile, hf = i % GT, i // GT
                    c = slice(tile * S + hf * 512, tile * S + (hf + 1) * 512)
                    n = 6 * g + i + 1
                    dve.wait_ge(i_sig, n)
                    k = TT(uc[:, c], uc[:, c], ti, ALU.mult)
                    k.then_inc(psum_free, 2)
                    if i:
                        dve.wait_ge(y_ready, n - 1)
                    dve.wait_ge(r_tanh, n)
                    link(TS(t(2), tr, 1.0, None, ALU.add))
                    link(nc.vector.reciprocal(t(2), t(2)))
                    dve.wait_ge(t_root, n)
                    STT(tr, tr, 1.0, t(2), ALU.subtract, ALU.mult, reverse0=True)
                    link(STT(ti, ti, 2.0, t(2), ALU.mult, ALU.mult))
                    link(TT(uc[:, c], uc[:, c], ti, ALU.mult))
                    start = uc[:, tile * S + 511:tile * S + 512] if hf else 0.0
                    k = nc.vector.tensor_tensor_scan(uc[:, c], tr, uc[:, c], start, ALU.mult, ALU.add)
                    k.then_inc(l_scan, 1)
                    dve.wait_ge(l_scan, n)
                    TT(t(2), uc[:, c], R3[:, c], ALU.mult).then_inc(y_out, 1)
                    dve.wait_ge(y_rounded, n)
                    TT(a_lo[:, c], t(2), a_hi[:, c].bitcast(F32), ALU.subtract).then_inc(y_ready, 1)

            conv(0, JB_LRU, 0)
            gelu_seen(0, 6)
            u_split(0)
            gate_chain(0)
            with dve.Fori(1, GROUPS) as g:
                base = JB_LRU + L_FIRST + (g - 1) * L_TURN
                step.n -= 1 + 3 * 3 + 6 * 4
                step.loop(g, 1 + 3 * 3 + 6 * 4)
                conv(g, base, 0)
                gelu_seen(g, 6)
                for nh in range(2):
                    for s in range(SB):
                        add(base + 12 + nh * 8 + s, 12 + nh * 8 + s, s, nh)
                u_split(g)
                gate_chain(g)
            step.end(GROUPS)
            for nh in range(2):
                for s in range(SB):
                    add(JB_LRU + L_FIRST + (GROUPS - 1) * L_TURN + nh * 8 + s, nh * 8 + s, s, nh)
            norm(3)
            ffn(1)
            fn = scr[:, 0:D]
            dve.wait_ge(n_sq, 8 * 5)
            TS(ssq[:], ssq[:], 1.0 / D, EPS, ALU.mult, ALU.add).then_inc(n_var, 1)
            dve.wait_ge(n_root, 9)
            link(nc.vector.reciprocal(rstd[:], rstd[:]))
            dve.wait_ge(fn_in, 16)
            for s in range(SB):
                STT(xn[:, s * D:(s + 1) * D], X[:, s * D:(s + 1) * D], rstd[:, s:s + 1], fn,
                    ALU.mult, ALU.mult).then_inc(out_ready, 1)


INS = ["x", "positions", "mix_norm", "ffn_norm", "final_norm", "ret_w_in", "ret_w_out", "lru_w_in",
       "lru_conv_w", "lru_conv_b", "lru_w_r", "lru_b_r", "lru_w_i", "lru_b_i", "lru_lambda", "lru_w_out",
       "ffn_w_gu", "ffn_w_down"]


def constants():
    import numpy as np
    freq = np.float32(10000.0) ** (-np.arange(P, dtype=np.float32) * np.float32(2.0) / np.float32(DK))
    log_gamma = np.log1p(-(2.0 ** (-5.0 - np.arange(HEADS, dtype=np.float64))))
    rel = np.arange(S, dtype=np.float64)[None, :] - np.arange(P, dtype=np.float64)[:, None]
    table = np.where(rel >= 0, np.exp(np.maximum(rel, 0.0) * log_gamma[:, None, None]), 0.0) * DK ** -0.5
    return {"inv_freq": freq.reshape(P, 1).astype(np.float32), "decay": table.astype(np.float32)}


def kernel(**inputs):
    import numpy as np
    import concourse.bacc as bacc
    from concourse.bass_utils import run_bass_kernel_spmd

    nc = bacc.Bacc("TRN2", target_bir_lowering=False, num_devices=1)
    arrays, args = {}, []
    given = {name: np.ascontiguousarray(inputs[name]) for name in INS}
    for name, a in {**given, **constants()}.items():
        arrays[f"in_{name}"] = a
        args.append(nc.dram_tensor(f"in_{name}", a.shape, mybir.dt.from_np(a.dtype), kind="ExternalInput").ap())
    y = nc.dram_tensor("out_y", (1, S, D), F32, kind="ExternalOutput").ap()
    build(nc, *args, y)
    r = run_bass_kernel_spmd(nc, [arrays], core_ids=[0])
    return r.results[0]["out_y"]
```

```python
from contextlib import ExitStack

import concourse.bass as bass
from concourse import mybir
from concourse.alu_op_type import AluOpType as ALU

ACT = mybir.ActivationFunctionType
AX_X = mybir.AxisListType.X
F32 = mybir.dt.float32
F32R = mybir.dt.float32r
I32 = mybir.dt.int32

P = 128
D = 1024
S = 1024
KT = D // P
SB = S // P
BANK = 512
EPS = 1e-6
HEADS = 4
DK = D // HEADS
DV = 2 * D // HEADS
LRU = 1536
BLOCK_W = LRU // 8
GT = 3
GROUPS = LRU // (GT * P)
FFN = 2816
CT = 2
CHUNKS = FFN // (CT * P)
RING = 3

SCORES = ([(c, P * c, BANK - P * c) for c in range(4)]
          + [(c, q, 256) for c in range(4) for q in (512, 768)]
          + [(c, P * c, S - P * c) for c in range(4, 8)])
SCORE_AT = [sum(n for _, _, n in SCORES[:i]) for i in range(len(SCORES))]
SCORE_COLS = sum(n for _, _, n in SCORES)
MEETS = [(0, 1), (0, 1, 2), (1, 2)]

J_QK, J_G, J_S, J_V, J_O, J_T, J_W = 0, 8, 16, 32, 40, 48, 56
HEAD_JOBS = 72
CHUNK_JOBS = 24
NORM_JOBS = 16
JB_NORM = [0]
JB_RET = NORM_JOBS
JB_NORM.append(JB_RET + HEADS * HEAD_JOBS)
JB_FFN = [JB_NORM[1] + NORM_JOBS]
JB_NORM.append(JB_FFN[0] + CHUNKS * CHUNK_JOBS)
JB_LRU = JB_NORM[2] + NORM_JOBS
L_FIRST, L_TURN, L_LAST = 24, 40, 16
JB_NORM.append(JB_LRU + L_FIRST + (GROUPS - 1) * L_TURN + L_LAST)
JB_FFN.append(JB_NORM[3] + NORM_JOBS)
JOBS = JB_FFN[1] + CHUNKS * CHUNK_JOBS

L_OUT, L_RI, L_RI_LAST = 12, 28, 20

HEAD_UNITS, CHUNK_UNITS = 32, 12
UB_FFN = [HEADS * HEAD_UNITS]
UB_LRU = UB_FFN[0] + CHUNKS * CHUNK_UNITS
UB_FFN.append(UB_LRU + GROUPS * 18)
UNITS = UB_FFN[1] + CHUNKS * CHUNK_UNITS

C_MIX, C_FFN, C_CONV, C_CONVB, C_BR, C_BI, C_LAM = 0, 16, 32, 80, 92, 104, 116


class Tally:

    def __init__(self, sem):
        self.sem, self.base, self.n, self.turn, self.per = sem, 0, 0, None, 0

    def loop(self, turn, per):
        self.turn, self.per, self.start = turn, per, self.n

    def end(self, turns):
        assert self.n - self.start == self.per, (self.n - self.start, self.per)
        self.n = self.start + self.per * turns
        self.turn = None

    def up(self, ins):
        self.n += 1
        ins.then_inc(self.sem, 1)
        return ins

    def now(self):
        return self.n if self.turn is None else self.turn * self.per + self.n


def build(nc, x, positions, mix_norm, ffn_norm, final_norm, ret_w_in, ret_w_out, lru_w_in, lru_conv_w,
          lru_conv_b, lru_w_r, lru_b_r, lru_w_i, lru_b_i, lru_lambda, lru_w_out, ffn_w_gu, ffn_w_down,
          inv_freq, decay, out):
    ctx = ExitStack()
    with ctx:
        def sb(name, cols, dt=F32, stack=ctx):
            return stack.enter_context(nc.sbuf_tensor(name, [P, cols], dt))

        def sem(name):
            return ctx.enter_context(nc.semaphore(name))

        X = sb("residual", SB * D)
        h_hi, h_lo = sb("h_hi", KT * S, F32R), sb("h_lo", KT * S, F32R)
        raw = sb("w_raw", RING * 512)
        w_hi, w_lo = sb("w_hi", RING * 512, F32R), sb("w_lo", RING * 512, F32R)
        T = sb("tmp", 3 * 512)
        R3 = sb("gate_buf", 8 * 512)
        dk = sb("decay_sb", 520)
        ident = sb("ident", P)
        cols = sb("cols", P)
        gc_conv, gc_gate = sb("gc_conv", 24), sb("gc_gate", 24)
        ssq, rstd, invf, small = sb("ssq", 8), sb("rstd", 8), sb("invf", 1), sb("small", 72)
        with ExitStack() as one:
            xn = sb("xn", SB * D, F32, one)
        a_hi, a_lo = sb("a_hi", 4096, F32R), sb("a_lo", 4096, F32R)
        with ExitStack() as one:
            wri_hi, wri_lo = sb("wri_hi", 2304, F32R, one), sb("wri_lo", 2304, F32R, one)
            uc, wri_raw = sb("uc", 3072, F32, one), sb("wri_raw", 1152, F32, one)
        with ExitStack() as one:
            scr = sb("scratch", 9216, F32, one)
        with ExitStack() as one:
            pos = sb("pos", 1024, I32, one)
            turns_i = sb("turns_i", 1024, I32, one)
        b_hi, b_lo = sb("b_hi", SCORE_COLS, F32R), sb("b_lo", SCORE_COLS, F32R)
        assert SCORE_COLS == 4608
        ps = ctx.enter_context(nc.psum_tensor("ps", [P, 8 * BANK], F32))
        rope_dram = nc.dram_tensor("rope_tables", (2, P, S), F32, kind="Internal").ap()

        def bank(e, a=0, n=BANK):
            return ps[:, (e % 8) * BANK + a:(e % 8) * BANK + a + n]

        def t(i):
            return T[:, i * 512:(i + 1) * 512]

        def r3(i, n=1):
            return R3[:, i * 512:(i + n) * 512]

        spare = [xn[:, c:c + 512] for c in (GT * S, GT * S + 512, 4096 + GT * S)]
        r_buf = (t(0), r3(6), dk[:, 0:512], spare[0])
        i_buf = (t(1), spare[1], spare[2])
        s_buf = (r3(7), t(2))

        x_in = [sem(f"x_in{i}") for i in range(SB)]
        vec_in, pos_in, fn_in = sem("vec_in"), sem("pos_in"), sem("fn_in")
        raw_in = [sem(f"raw_in{i}") for i in range(RING)]
        w_rounded, w_ready, w_begun = sem("w_rounded"), sem("w_ready"), sem("w_begun")
        ident_ready, vec_T, cols_ready = sem("ident_ready"), sem("vec_T"), sem("cols_ready")
        psum_full, psum_free = sem("psum_full"), sem("psum_free")
        dve_step, act_step = sem("dve_step"), sem("act_step")
        n_sq, n_var, n_root, xn_ready, h_rounded = (
            sem("n_sq"), sem("n_var"), sem("n_root"), sem("xn_ready"), sem("h_rounded"))
        table_arg, table_out, rope_saved = sem("table_arg"), sem("table_out"), sem("rope_saved")
        rope_in, decay_in = sem("rope_in"), sem("decay_in")
        rope_out, qk_rounded, qk_ready = sem("rope_out"), sem("qk_rounded"), sem("qk_ready")
        s_rounded, s_ready = sem("s_rounded"), sem("s_ready")
        g_sig = sem("g_sig")
        v_rounded = sem("v_rounded")
        o_sq, o_var, o_root, o_ready = sem("o_sq"), sem("o_var"), sem("o_root"), sem("o_ready")
        ot_rounded = sem("ot_rounded")
        f_sig, f_rounded, f_ready = sem("f_sig"), sem("f_rounded"), sem("f_ready")
        lam_e, lam_sp = sem("lam_e"), sem("lam_sp")
        wri_in, wri_zero, wri_round, wri_ready = (
            sem("wri_in"), sem("wri_zero"), sem("wri_round"), sem("wri_ready"))
        u_rounded, u_ready = sem("u_rounded"), sem("u_ready")
        gelu_done, gc_ready = sem("gelu_done"), sem("gc_ready")
        r_sig, i_sig, r_tanh, a_exp, t_root = (
            sem("r_sig"), sem("i_sig"), sem("r_tanh"), sem("a_exp"), sem("t_root"))
        l_scan, y_out, y_rounded, y_ready = (
            sem("l_scan"), sem("y_out"), sem("y_rounded"), sem("y_ready"))
        out_ready, out_done = sem("out_ready"), sem("out_done")
        block = ctx.enter_context(nc.Block())

        @block.sync
        def _(sp):
            vec = scr[:, 8 * 1024:8 * 1024 + P]
            for at, n, src in ((C_MIX, 16, mix_norm.rearrange("l (k p) -> (l k) p", p=P)),
                               (C_FFN, 16, ffn_norm.rearrange("l (k p) -> (l k) p", p=P)),
                               (C_CONV, 48, lru_conv_w[0].rearrange("j (k p) -> (j k) p", p=P)),
                               (C_CONVB, 12, lru_conv_b[0].rearrange("(k p) -> k p", p=P)),
                               (C_BR, 12, lru_b_r[0].rearrange("b c -> (b c)").rearrange("(k p) -> k p", p=P)),
                               (C_BI, 12, lru_b_i[0].rearrange("b c -> (b c)").rearrange("(k p) -> k p", p=P)),
                               (C_LAM, 12, lru_lambda[0].rearrange("(k p) -> k p", p=P))):
                sp.dma_start(vec[at:at + n, :], src).then_inc(vec_in, 16)
            sp.dma_start(pos[:], positions.to_broadcast([P, S])).then_inc(pos_in, 16)
            sp.dma_start(invf[:], inv_freq).then_inc(pos_in, 16)
            for s in range(SB):
                sp.dma_start(X[:, s * D:(s + 1) * D], x[0, s * P:(s + 1) * P, :]).then_inc(x_in[s], 16)

            def load(slot, src, ready):
                if ready is not None:
                    sp.wait_ge(w_ready, ready)
                dst = raw[:, slot * 512:(slot + 1) * 512]
                if len(src.shape) == 3:
                    dst = dst.rearrange("p (k n) -> p k n", k=4)
                sp.dma_start(dst, src).then_inc(raw_in[slot], 16)

            def rows(w, kh, col):
                return w[kh * 512:(kh + 1) * 512, bass.ds(col, P)].rearrange("(k p) n -> p k n", p=P)

            def last(u, j, restart):
                return u - 1 if restart and j < 2 else u - 2

            def head(h, first):
                for j in range(HEAD_UNITS):
                    if j < 8:
                        tile, kh = j // 2, j % 2
                        src = rows(ret_w_in[0], kh, (tile // 2) * D + h * DK + (tile % 2) * P)
                    elif j < 24:
                        k = (j - 8) % 8
                        off = (2 * D + HEADS * DV) if j < 16 else 2 * D
                        src = ret_w_in[0][k * P:(k + 1) * P, bass.ds(off + h * DV, DV)]
                    else:
                        nh, k = (j - 24) // 4, (j - 24) % 4
                        src = ret_w_out[0][bass.ds(h * DV + k * P, P), nh * 512:(nh + 1) * 512]
                    load(j % RING, src, None if first and j < RING else
                         last(h * HEAD_UNITS + j, j, not first))
            head(0, True)
            with sp.Fori(1, HEADS) as h:
                head(h, False)

            def ffn(layer):
                def chunk(c, restart):
                    for j in range(CHUNK_UNITS):
                        if j < 8:
                            tile, up, kh = j // 4, (j // 2) % 2, j % 2
                            src = rows(ffn_w_gu[layer], kh, up * FFN + c * (CT * P) + tile * P)
                        else:
                            nh, k = (j - 8) // 2, j % 2
                            src = ffn_w_down[layer][bass.ds(c * (CT * P) + k * P, P), nh * 512:(nh + 1) * 512]
                        load(j % RING, src, last(UB_FFN[layer] + c * CHUNK_UNITS + j, j, restart))
                chunk(0, layer == 0)
                with sp.Fori(1, CHUNKS) as c:
                    chunk(c, False)

            ffn(0)

            def gates(g, w, n, behind=None):
                sp.wait_ge(wri_ready, n)
                sp.wait_ge(wri_zero, 1)
                a = w[0][bass.ds(2 * g, 1)].rearrange("a c d -> (a c) d")
                b = w[0][bass.ds(2 * g + 1, 1)].rearrange("a c d -> (a c) d")
                r = wri_raw
                pieces = ((r[:, 0:192], a[0:128, :]), (r[0:64, 384:576], a[128:192, :]),
                          (r[64:128, 576:768], b[0:64, :]), (r[:, 960:1152], b[64:192, :]))
                for dst, src in pieces:
                    if behind is not None and dst is pieces[-1][0]:
                        sp.wait_ge(w_ready, behind)
                    sp.dma_start(dst, src).then_inc(wri_in, 16)

            def into(g, gate, u0, waited=False):
                for j in range(6):
                    tile, kh = j // 2, j % 2
                    src = rows(lru_w_in[0], kh, (0 if gate else LRU) + g * (GT * P) + tile * P)
                    load(j % RING, src, None if waited and j == 0 else last(u0 + j, j, False))

            def outof(g, u0):
                for j in range(6):
                    nh, k = j // 3, j % 3
                    src = lru_w_out[0][bass.ds(g * (GT * P) + k * P, P), nh * 512:(nh + 1) * 512]
                    load(j % RING, src, last(u0 + j, j, False))

            into(0, False, UB_LRU)
            gates(0, lru_w_r, 0)
            into(0, True, UB_LRU + 6)
            gates(0, lru_w_i, 1)
            with sp.Fori(1, GROUPS) as g:
                u0 = UB_LRU + g * 18 - 6
                into(g, False, u0)
                gates(g, lru_w_r, 2 * g, last(u0 + 6, 0, False))
                into(g, True, u0 + 6, waited=True)
                gates(g, lru_w_i, 2 * g + 1)
                outof(g - 1, u0 + 12)
            outof(GROUPS - 1, UB_LRU + GROUPS * 18 - 6)
            ffn(1)
            sp.wait_ge(psum_free, JB_NORM[3])
            sp.dma_start(scr[:, 0:D], final_norm.rearrange("(a n) -> a n", a=1).to_broadcast([P, D]))\
              .then_inc(fn_in, 16)
            for s in range(SB):
                sp.wait_ge(out_ready, s + 1)
                sp.dma_start(out[0, s * P:(s + 1) * P, :], xn[:, s * D:(s + 1) * D]).then_inc(out_done, 16)
            sp.wait_ge(out_done, 16 * SB)

        @block.gpsimd
        def _(pool):
            nc.gpsimd.memset(ident[:], 0.0).then_inc(ident_ready, 1)
            pool.wait_ge(ident_ready, 1)
            nc.gpsimd.affine_select(out=ident[:], in_=ident[:], compare_op=ALU.not_equal, fill=1.0, base=0,
                                    pattern=[[-1, P]], channel_multiplier=1).then_inc(ident_ready, 1)

            def touch(col):
                nc.gpsimd.tensor_tensor(small[:, 62:63], col, col, ALU.subtract)

            def split(slot, loads, u, used):
                cut = slice(slot * 512, (slot + 1) * 512)
                pool.wait_ge(raw_in[slot], loads)
                if used is not None:
                    pool.wait_ge(w_begun, used)
                touch(raw[:, slot * 512:slot * 512 + 1])
                nc.gpsimd.tensor_copy(w_hi[:, cut], raw[:, cut]).then_inc(w_rounded, 1)
                pool.wait_ge(w_rounded, u + 1)
                nc.gpsimd.tensor_tensor(w_lo[:, cut], raw[:, cut], w_hi[:, cut].bitcast(F32),
                                        ALU.subtract).then_inc(w_ready, 1)

            def head(h, first):
                for j in range(HEAD_UNITS):
                    u, slot = h * HEAD_UNITS + j, j % RING
                    used = None if first and j < RING else u if j < 2 else u - 1
                    split(slot, 16 * (h * (11 if slot < 2 else 10) + j // RING + 1), u, used)
            head(0, True)
            with pool.Fori(1, HEADS) as h:
                head(h, False)
            landed = [HEADS * (11 if slot < 2 else 10) for slot in range(RING)]

            def units(n, u0, before, restart=False):
                for j in range(n):
                    split(j % RING, 16 * (before[j % RING] + j // RING + 1), u0 + j,
                          u0 + j - (0 if restart and j < 2 else 1))

            def ffn(layer, landed):
                def chunk(c, restart):
                    units(CHUNK_UNITS, UB_FFN[layer] + c * CHUNK_UNITS, [c * 4 + n for n in landed], restart)
                chunk(0, layer == 0)
                with pool.Fori(1, CHUNKS) as c:
                    chunk(c, False)

            ffn(0, landed)
            landed = [n + 4 * CHUNKS for n in landed]
            pool.wait_ge(psum_full, JB_LRU)
            nc.gpsimd.memset(wri_raw[:], 0.0).then_inc(wri_zero, 1)

            def gates(g, n, at):
                pool.wait_ge(wri_in, 64 * (n + 1))
                touch(wri_raw[:, 0:1])
                cut = slice(at * 1152, (at + 1) * 1152)
                nc.gpsimd.tensor_copy(wri_hi[:, cut], wri_raw[:]).then_inc(wri_round, 1)
                pool.wait_ge(wri_round, n + 1)
                nc.gpsimd.tensor_tensor(wri_lo[:, cut], wri_raw[:], wri_hi[:, cut].bitcast(F32),
                                        ALU.subtract).then_inc(wri_ready, 1)

            units(6, UB_LRU, landed)
            gates(0, 0, 0)
            units(6, UB_LRU + 6, [n + 2 for n in landed])
            gates(0, 1, 1)
            with pool.Fori(1, GROUPS) as g:
                u0 = UB_LRU + g * 18 - 6
                now = [n + g * 6 - 2 for n in landed]
                units(6, u0, now)
                pool.wait_ge(psum_full, JB_LRU + L_FIRST + (g - 1) * L_TURN + 1)
                gates(g, 2 * g, 0)
                units(6, u0 + 6, [n + 2 for n in now])
                gates(g, 2 * g + 1, 1)
                units(6, u0 + 12, [n + 4 for n in now])
            units(6, UB_LRU + GROUPS * 18 - 6, [n + GROUPS * 6 - 2 for n in landed])
            ffn(1, [n + GROUPS * 6 for n in landed])

        @block.tensor
        def _(pe):
            def free(e):
                pe.wait_ge(psum_free, e - 7)

            def three(o, l_hi, l_lo, r_hi, r_lo, start, stop, begins=False):
                m = nc.tensor.matmul(o, l_hi, r_hi, start=start, stop=False)
                if begins:
                    m.then_inc(w_begun, 1)
                nc.tensor.matmul(o, l_hi, r_lo, start=False, stop=False)
                return nc.tensor.matmul(o, l_lo, r_hi, start=False, stop=stop)

            def rows_unit(j, u, kh, banks):
                pe.wait_ge(w_ready, u + 1)
                for kk in range(4):
                    w = slice((j % RING) * 512 + kk * P, (j % RING) * 512 + (kk + 1) * P)
                    for hf in range(2):
                        r = slice((kh * 4 + kk) * S + hf * 512, (kh * 4 + kk) * S + (hf + 1) * 512)
                        m = three(bank(banks[hf]), w_hi[:, w], w_lo[:, w], h_hi[:, r], h_lo[:, r],
                                  kh == 0 and kk == 0, kh == 1 and kk == 3, kk == 0 and hf == 0)
                        if kh == 1 and kk == 3:
                            m.then_inc(psum_full, 1)

            def cols_unit(j, u, k, nk, l_hi, l_lo, at, e0, base, ready=None):
                pe.wait_ge(w_ready, u + 1)
                w = slice((j % RING) * 512, (j % RING + 1) * 512)
                for s in range(SB):
                    if k == 0:
                        free(base + e0 + s)
                    if ready is not None:
                        pe.wait_ge(ready[0], ready[1](s))
                    c = at + s * P
                    m = three(bank(e0 + s), l_hi[:, c:c + P], l_lo[:, c:c + P], w_hi[:, w], w_lo[:, w],
                              k == 0, k == nk - 1, s == 0)
                    if k == nk - 1:
                        m.then_inc(psum_full, 1)

            def tile_rows(j, u, base, banks, wait, norm=None):
                free(base + wait)
                if norm is not None:
                    pe.wait_ge(psum_free, JB_NORM[norm] + 8)
                rows_unit(j, u, 0, banks)
                if norm is not None:
                    pe.wait_ge(psum_free, JB_NORM[norm] + 16)
                rows_unit(j + 1, u + 1, 1, banks)

            def norm(n):
                for k in range(KT):
                    for hf in range(2):
                        e = JB_NORM[n] + 2 * k + hf
                        if e >= 8:
                            free(e)
                        for s in range(4):
                            if k == 0:
                                pe.wait_ge(xn_ready, 8 * n + hf * 4 + s + 1)
                            c = (hf * 4 + s) * D + k * P
                            m = nc.tensor.transpose(bank(e, s * P, P), xn[:, c:c + P], ident[:])
                        m.then_inc(psum_full, 1)

            pe.wait_ge(vec_in, 16 * 7)
            pe.wait_ge(ident_ready, 2)
            nc.tensor.transpose(ps[:, 7 * BANK:7 * BANK + P], scr[:, 8 * 1024:8 * 1024 + P],
                                ident[:]).then_inc(vec_T, 1)
            pe.wait_ge(cols_ready, 1)
            norm(0)

            with pe.Fori(0, HEADS) as h:
                base, ub = JB_RET + h * HEAD_JOBS, h * HEAD_UNITS
                for tile in range(4):
                    b = 4 * (tile // 2) + tile % 2
                    tile_rows(2 * tile, ub + 2 * tile, base, (b, b + 2), b + 2, 0 if tile == 0 else None)
                for k in range(KT):
                    cols_unit(8 + k, ub + 8 + k, k, KT, h_hi, h_lo, k * S, J_G, base)
                for i, (c, q, n) in enumerate(SCORES):
                    if i == 0:
                        pe.wait_ge(qk_ready, h * 8 + 8)
                    free(base + J_S + i)
                    for d in range(2):
                        kc, qc = (2 + d) * S + c * P, d * S + q
                        m = three(bank(J_S + i, 0, n), a_hi[:, kc:kc + P], a_lo[:, kc:kc + P],
                                  a_hi[:, qc:qc + n], a_lo[:, qc:qc + n], d == 0, d == 1)
                    m.then_inc(psum_full, 1)
                for k in range(KT):
                    cols_unit(16 + k, ub + 16 + k, k, KT, h_hi, h_lo, k * S, J_V, base)
                pe.wait_ge(s_ready, h * 16 + 16)
                for s in range(SB):
                    free(base + J_O + s)
                    pe.wait_ge(psum_free, base + J_V + s + 1)
                    for c in range(s + 1):
                        i = next(i for i, (cc, q, n) in enumerate(SCORES) if cc == c and q <= s * P < q + n)
                        a = SCORE_AT[i] + s * P - SCORES[i][1]
                        m = three(bank(J_O + s), b_hi[:, a:a + P], b_lo[:, a:a + P],
                                  a_hi[:, c * 512:(c + 1) * 512], a_lo[:, c * 512:(c + 1) * 512],
                                  c == 0, c == s)
                    m.then_inc(psum_full, 1)
                for s in range(SB):
                    free(base + J_T + s)
                    pe.wait_ge(o_ready, h * 8 + s + 1)
                    for d in range(4):
                        m = nc.tensor.transpose(bank(J_T + s, d * P, P),
                                                R3[:, s * 512 + d * P:s * 512 + (d + 1) * P], ident[:])
                    m.then_inc(psum_full, 1)
                for nh in range(2):
                    for k in range(4):
                        j = 24 + nh * 4 + k
                        cols_unit(j, ub + j, k, 4, b_hi, b_lo, k * S, J_W + nh * 8, base,
                                  (psum_free, lambda s: base + J_T + s + 1) if nh == 0 and k == 0 else None)

            def ffn(layer):
                with pe.Fori(0, CHUNKS) as c:
                    base, ub = JB_FFN[layer] + c * CHUNK_JOBS, UB_FFN[layer] + c * CHUNK_UNITS
                    for i in range(4):
                        b = 4 * (i // 2) + i % 2
                        tile_rows(2 * i, ub + 2 * i, base, (b, b + 2), b + 2, 2 * layer + 1 if i == 0 else None)
                    for nh in range(2):
                        for k in range(CT):
                            if nh == 0:
                                pe.wait_ge(f_ready, (layer * CHUNKS + c) * 4 + 2 * k + 2)
                            j = 8 + nh * 2 + k
                            cols_unit(j, ub + j, k, CT, a_hi, a_lo, k * S, 8 + nh * 8, base)

            norm(1)
            ffn(0)
            norm(2)

            def lru_into(u0, base, e0):
                for tile in range(GT):
                    e = e0 + 2 * tile
                    tile_rows(2 * tile, u0 + 2 * tile, base, (e, e + 1), e + 1, 2 if e == 0 else None)

            def lru_gates(g, base, e0, u_hi, u_lo):
                pe.wait_ge(wri_ready, 2 * g + 2)
                for hf in range(2):
                    for tile in range(GT):
                        for m_i in range(2):
                            e = e0 + (hf * GT + tile) * 2 + m_i
                            free(base + e)
                            if hf == 0 and m_i == 0 and tile < 2:
                                pe.wait_ge(u_ready, 3 * g + 2 + tile)
                            for kt in MEETS[tile]:
                                w = slice(m_i * 1152 + kt * 384 + tile * P, m_i * 1152 + kt * 384 + (tile + 1) * P)
                                r = slice(kt * S + hf * 512, kt * S + (hf + 1) * 512)
                                m = three(bank(e), wri_hi[:, w], wri_lo[:, w], u_hi[:, r], u_lo[:, r],
                                          kt == MEETS[tile][0], kt == MEETS[tile][-1])
                            m.then_inc(psum_full, 1)

            def lru_outof(g, u0, base, e0, nh, y_hi, y_lo):
                for k in range(GT):
                    j = nh * 3 + k
                    if nh == 0:
                        pe.wait_ge(y_ready, g * 6 + k + 4)
                    cols_unit(j, u0 + j, k, GT, y_hi, y_lo, k * S, e0, base)

            lru_into(UB_LRU, JB_LRU, 0)
            lru_into(UB_LRU + 6, JB_LRU, 6)
            lru_gates(0, JB_LRU, 12, a_hi, a_lo)
            with pe.Fori(1, GROUPS - 1) as g:
                base, u0 = JB_LRU + L_FIRST + (g - 1) * L_TURN, UB_LRU + g * 18 - 6
                lru_into(u0, base, 0)
                lru_into(u0 + 6, base, 6)
                for nh in range(2):
                    lru_outof(g - 1, u0 + 12, base, L_OUT + 8 * nh, nh, a_hi, a_lo)
                lru_gates(g, base, L_RI, a_hi, a_lo)
            base, u0 = JB_LRU + L_FIRST + (GROUPS - 2) * L_TURN, UB_LRU + (GROUPS - 1) * 18 - 6
            lru_into(u0, base, 0)
            lru_into(u0 + 6, base, 6)
            lru_outof(GROUPS - 2, u0 + 12, base, L_OUT, 0, a_hi, a_lo)
            lru_gates(GROUPS - 1, base, L_RI_LAST, h_hi, h_lo)
            lru_outof(GROUPS - 2, u0 + 12, base, L_RI_LAST + 12, 1, a_hi, a_lo)
            for nh in range(2):
                lru_outof(GROUPS - 1, u0 + 18, base + L_TURN, 8 * nh, nh, h_hi, h_lo)
            norm(3)
            ffn(1)

        @block.scalar
        def _(act):
            def full(e):
                act.wait_ge(psum_full, e + 1)

            def square_rows(s, n):
                junk = s % 4 * D
                nc.scalar.activation(R3[:, junk:junk + D], X[:, s * D:(s + 1) * D], ACT.Square,
                                     accum_out=ssq[:, s:s + 1]).then_inc(n_sq, 1)

            def block_ready(n, e, s):
                act.wait_ge(psum_free, e - 7 + s)
                if s >= 4:
                    act.wait_ge(n_sq, 8 * n + s - 3)

            def load_sqrt():
                nc.scalar.activation(small[:, 71:72], ident[:, 0:1], ACT.Sqrt)

            def norm(n):
                if n:
                    load_sqrt()
                for hf in range(2):
                    for s in range(hf * 4, hf * 4 + 4):
                        if n == 0:
                            act.wait_ge(x_in[s], 16)
                            if s >= 4:
                                act.wait_ge(n_sq, s - 3)
                        else:
                            block_ready(n, JB_NORM[n], s)
                        square_rows(s, n)
                    act.wait_ge(n_var, 2 * n + hf + 1)
                    nc.scalar.activation(rstd[:, hf * 4:hf * 4 + 4], ssq[:, hf * 4:hf * 4 + 4],
                                         ACT.Sqrt).then_inc(n_root, 1)
                if n == 0:
                    act.wait_ge(cols_ready, 1)
                for k in range(KT):
                    for hf in range(2):
                        e = JB_NORM[n] + 2 * k + hf
                        full(e)
                        g = (C_MIX + (n // 2) * 8 if n % 2 == 0 else C_FFN + (n // 2) * 8) + k
                        nc.scalar.activation(h_hi[:, k * S + hf * 512:k * S + (hf + 1) * 512], bank(e),
                                             ACT.Copy, scale=cols[:, g:g + 1]).then_inc(h_rounded, 1)

            norm(0)
            for i in range(2):
                act.wait_ge(table_arg, i + 1)
                nc.scalar.activation(scr[:, (4 + i) * S:(5 + i) * S], scr[:, (2 + i) * S:(3 + i) * S],
                                     ACT.Sin).then_inc(table_out, 1)
                act.wait_ge(table_out, i + 1)
                act.dma_start(rope_dram[i], scr[:, (4 + i) * S:(5 + i) * S]).then_inc(rope_saved, 16)
            act.wait_ge(lam_e, 1)
            nc.scalar.activation(small[:, 12:24], small[:, 0:12], ACT.Exp).then_inc(lam_sp, 1)
            act.wait_ge(rope_saved, 32)

            with act.Fori(0, HEADS) as h:
                base = JB_RET + h * HEAD_JOBS
                act.wait_ge(psum_full, base)
                act.dma_start(R3[:, 0:S], rope_dram[1]).then_inc(rope_in, 16)
                act.dma_start(R3[:, S:2 * S], rope_dram[0]).then_inc(rope_in, 16)
                act.dma_start(dk[:], decay[bass.ds(h, 1)].rearrange("a p n -> (a p) n")).then_inc(decay_in, 16)
                for i in range(8):
                    pair, hf, d = i // 4, (i // 2) % 2, i % 2
                    act.wait_ge(rope_out, h * 8 + i + 1)
                    c = (2 * pair + d) * S + hf * 512
                    nc.scalar.activation(a_hi[:, c:c + 512], (t(0), t(1), t(2), r3(7))[i % 4], ACT.Copy)\
                        .then_inc(qk_rounded, 1)
                for s in range(SB):
                    full(base + J_G + s)
                    if s == 0:
                        act.wait_ge(qk_ready, h * 8 + 8)
                    if s >= 3:
                        act.wait_ge(psum_free, base + J_G + s - 2)
                    nc.scalar.activation(t(s % 3), bank(J_G + s), ACT.Sigmoid).then_inc(g_sig, 1)
                for i, (c, q, n) in enumerate(SCORES):
                    act.wait_ge(psum_free, base + J_S + i + 1)
                    nc.scalar.activation(b_hi[:, SCORE_AT[i]:SCORE_AT[i] + n], T[:, (i % 3) * 512:(i % 3) * 512 + n],
                                         ACT.Copy).then_inc(s_rounded, 1)
                for s in range(SB):
                    full(base + J_V + s)
                    nc.scalar.activation(a_hi[:, s * 512:(s + 1) * 512], bank(J_V + s), ACT.Copy)\
                        .then_inc(v_rounded, 1)
                act.wait_ge(s_ready, h * 16 + 16)
                load_sqrt()
                for s in range(SB):
                    full(base + J_O + s)
                    if s >= 3:
                        act.wait_ge(o_sq, h * 8 + s - 2)
                    nc.scalar.activation(t(s % 3), bank(J_O + s), ACT.Square,
                                         accum_out=ssq[:, s:s + 1]).then_inc(o_sq, 1)
                act.wait_ge(o_var, h + 1)
                nc.scalar.activation(rstd[:], ssq[:], ACT.Sqrt).then_inc(o_root, 1)
                for s in range(SB):
                    full(base + J_T + s)
                    nc.scalar.activation(b_hi[:, 0:4096].rearrange("p (d n) -> p d n", d=4)[:, :, s * P:(s + 1) * P],
                                         bank(J_T + s).rearrange("p (d n) -> p d n", d=4), ACT.Copy)\
                        .then_inc(ot_rounded, 1)

            def ffn(layer):
                with act.Fori(0, CHUNKS) as c:
                    base, n = JB_FFN[layer] + c * CHUNK_JOBS, (layer * CHUNKS + c) * 4

                    def rounded(i):
                        act.wait_ge(psum_free, base + 2 * i + 2)
                        at = (i // 2) * S + (i % 2) * 512
                        nc.scalar.activation(a_hi[:, at:at + 512], r3(4 + i), ACT.Copy).then_inc(f_rounded, 1)

                    for tile in range(CT):
                        for hf in range(2):
                            i = tile * 2 + hf
                            act.wait_ge(psum_full, base + 4 * tile + hf + 1)
                            nc.scalar.activation(r3(i), bank(4 * tile + 2 * hf), ACT.Sigmoid).then_inc(f_sig, 1)
                        rounded(2 * tile)
                        rounded(2 * tile + 1)

            norm(1)
            ffn(0)
            norm(2)

            def gelu(g, base, e0):
                for tile in range(GT):
                    full(base + e0 + 2 * tile + 1)
                    act.wait_ge(y_ready, g * 6)
                    b = (e0 + 2 * tile) % 8 * BANK
                    nc.scalar.activation(R3[:, tile * S:(tile + 1) * S], ps[:, b:b + 2 * BANK],
                                         ACT.Gelu_apprx_tanh).then_inc(gelu_done, 1)

            def u_round(g, base, u_hi, begun=None, full_to=None):
                for tile in range(GT):
                    if begun is not None and tile < 2:
                        act.wait_ge(w_begun, begun + tile)
                    elif full_to is not None:
                        act.wait_ge(psum_full, full_to)
                    act.wait_ge(psum_free, base + 2 * tile + 2)
                    nc.scalar.activation(u_hi[:, tile * S:(tile + 1) * S], uc[:, tile * S:(tile + 1) * S],
                                         ACT.Copy).then_inc(u_rounded, 1)

            def gate_chain(g, base, e0, y_hi):
                def gates(i):
                    tile = i % GT
                    if i >= 4:
                        act.wait_ge(l_scan, 6 * g + i - 3)
                    full(base + e0 + 2 * i)
                    nc.scalar.activation(r_buf[i % 4], bank(e0 + 2 * i), ACT.Sigmoid,
                                         bias=gc_gate[:, 15 + tile:16 + tile]).then_inc(r_sig, 1)
                    full(base + e0 + 2 * i + 1)
                    if i >= 3:
                        act.wait_ge(psum_free, base + e0 + 2 * i - 4)
                    nc.scalar.activation(i_buf[i % 3], bank(e0 + 2 * i + 1), ACT.Sigmoid,
                                         bias=gc_gate[:, 18 + tile:19 + tile]).then_inc(i_sig, 1)

                def tanh_exp(items):
                    for i in items:
                        if i >= 2:
                            act.wait_ge(l_scan, 6 * g + i - 1)
                        act.wait_ge(r_sig, 6 * g + i + 1)
                        nc.scalar.activation(s_buf[i % 2], r_buf[i % 4], ACT.Tanh,
                                             scale=gc_gate[:, 21 + i % GT:22 + i % GT]).then_inc(r_tanh, 1)
                    for i in items:
                        act.wait_ge(r_tanh, 6 * g + i + 1)
                        nc.scalar.activation(r_buf[i % 4], r_buf[i % 4], ACT.Exp,
                                             scale=gc_gate[:, i % GT:i % GT + 1]).then_inc(a_exp, 1)

                def roots(items):
                    for i in items:
                        nc.scalar.activation(s_buf[i % 2], s_buf[i % 2], ACT.Sqrt).then_inc(t_root, 1)

                def y_round(items):
                    for i in items:
                        act.wait_ge(y_out, 6 * g + i + 1)
                        act.wait_ge(psum_full, base + e0 + (6 if i < GT else 12))
                        at = i % GT * S + i // GT * 512
                        nc.scalar.activation(y_hi[:, at:at + 512], R3[:, at:at + 512], ACT.Copy)\
                            .then_inc(y_rounded, 1)

                act.wait_ge(gc_ready, g + 1)
                gates(0)
                gates(1)
                tanh_exp((0, 1))
                roots((0, 1))
                gates(2)
                gates(3)
                y_round((0, 1))
                gates(4)
                gates(5)
                tanh_exp((2, 3))
                roots((2, 3))
                tanh_exp((4, 5))
                y_round((2, 3))
                roots((4, 5))
                y_round((4, 5))

            u_round(0, JB_LRU, a_hi)
            gelu(0, JB_LRU, 6)
            gate_chain(0, JB_LRU, 12, a_hi)
            with act.Fori(1, GROUPS - 1) as g:
                base = JB_LRU + L_FIRST + (g - 1) * L_TURN
                gelu(g, base, 6)
                u_round(g, base, a_hi, UB_LRU + g * 18 - 6 + 12 + GT + 2, base + L_RI)
                gate_chain(g, base, L_RI, a_hi)
            base = JB_LRU + L_FIRST + (GROUPS - 2) * L_TURN
            gelu(GROUPS - 1, base, 6)
            u_round(GROUPS - 1, base, h_hi, None, base + L_OUT)
            gate_chain(GROUPS - 1, base, L_RI_LAST, h_hi)
            norm(3)
            ffn(1)
            load_sqrt()
            for hf in range(2):
                for s in range(hf * 4, hf * 4 + 4):
                    block_ready(4, JOBS, s)
                    square_rows(s, 4)
                act.wait_ge(n_var, 8 + hf + 1)
                nc.scalar.activation(rstd[:, hf * 4:hf * 4 + 4], ssq[:, hf * 4:hf * 4 + 4],
                                     ACT.Sqrt).then_inc(n_root, 1)

        @block.vector
        def _(dve):
            step = Tally(dve_step)

            def link(ins):
                step.up(ins)
                dve.wait_ge(dve_step, step.now())

            def full(e):
                dve.wait_ge(psum_full, e + 1)

            TT, TS, STT = nc.vector.tensor_tensor, nc.vector.tensor_scalar, nc.vector.scalar_tensor_tensor

            def norm(n):
                for hf in range(2):
                    q = slice(hf * 4, hf * 4 + 4)
                    dve.wait_ge(n_sq, 8 * n + hf * 4 + 4)
                    TS(ssq[:, q], ssq[:, q], 1.0 / D, EPS, ALU.mult, ALU.add).then_inc(n_var, 1)
                    dve.wait_ge(n_root, 2 * n + hf + 1)
                    link(nc.vector.reciprocal(rstd[:, q], rstd[:, q]))
                    for s in range(hf * 4, hf * 4 + 4):
                        TS(xn[:, s * D:(s + 1) * D], X[:, s * D:(s + 1) * D], rstd[:, s:s + 1], None,
                           ALU.mult).then_inc(xn_ready, 1)
                for k in range(KT):
                    for hf in range(2):
                        e = JB_NORM[n] + 2 * k + hf
                        g = (C_MIX + (n // 2) * 8 if n % 2 == 0 else C_FFN + (n // 2) * 8) + k
                        c = slice(k * S + hf * 512, k * S + (hf + 1) * 512)
                        dve.wait_ge(h_rounded, 16 * n + 2 * k + hf + 1)
                        i = STT(h_lo[:, c], bank(e), cols[:, g:g + 1], h_hi[:, c].bitcast(F32),
                                ALU.mult, ALU.subtract)
                        i.then_inc(psum_free, 1)

            dve.wait_ge(vec_T, 1)
            nc.vector.tensor_copy(cols[:], ps[:, 7 * BANK:7 * BANK + P]).then_inc(cols_ready, 1)
            norm(0)

            dve.wait_ge(pos_in, 32)
            ang, tmp, rs, rc = (scr[:, i * S:(i + 1) * S] for i in (6, 7, 2, 3))
            link(nc.vector.tensor_copy(tmp, pos[:]))
            link(TS(ang, tmp, invf[:], None, ALU.mult))
            parts = (6.28125, 0.00193500518798828125, 3.01991598196e-07)
            for unit in (4096.0, 1.0):
                link(TS(tmp, ang, 1.0 / (6.283185307179586 * unit), None, ALU.mult))
                link(nc.vector.tensor_copy(turns_i[:], tmp))
                link(nc.vector.tensor_copy(tmp, turns_i[:]))
                for part in parts:
                    link(STT(ang, tmp, -part * unit, ang, ALU.mult, ALU.add))
            TS(rs, ang, 3.1415925, -3.1415925, ALU.min, ALU.max).then_inc(table_arg, 1)
            dve.wait_ge(table_arg, 1)
            link(STT(rc, rs, -1.0, rs, ALU.mult, ALU.max))
            TS(rc, rc, -1.0, 1.5707963267948966, ALU.mult, ALU.add).then_inc(table_arg, 1)
            lam = cols[:, C_LAM:C_LAM + 12]
            link(TS(small[:, 24:36], lam, -1.0, None, ALU.mult))
            TT(small[:, 0:12], lam, small[:, 24:36], ALU.min).then_inc(lam_e, 1)
            dve.wait_ge(lam_e, 1)
            link(TS(small[:, 24:36], small[:, 24:36], 0.0, None, ALU.max))
            dve.wait_ge(lam_sp, 1)
            z, zz, acc = small[:, 0:12], small[:, 36:48], small[:, 48:60]
            link(TS(z, small[:, 12:24], 2.0, None, ALU.add))
            link(nc.vector.reciprocal(z, z))
            link(TT(z, z, small[:, 12:24], ALU.mult))
            link(TT(zz, z, z, ALU.mult))
            link(TS(acc, zz, 1.0 / 17, 1.0 / 15, ALU.mult, ALU.add))
            for n in (13, 11, 9, 7, 5, 3, 1):
                link(TT(acc, acc, zz, ALU.mult))
                link(TS(acc, acc, 1.0 / n, None, ALU.add))
            link(TT(acc, acc, z, ALU.mult))
            link(STT(acc, acc, 2.0, small[:, 24:36], ALU.mult, ALU.add))
            link(TS(cols[:, C_LAM:C_LAM + 12], acc, 4.0, None, ALU.mult))

            def add(e, le, s, nh):
                c = slice(s * D + nh * 512, s * D + (nh + 1) * 512)
                full(e)
                TT(X[:, c], bank(le), X[:, c], ALU.add).then_inc(psum_free, 1)

            with dve.Fori(0, HEADS) as h:
                base = JB_RET + h * HEAD_JOBS
                step.loop(h, 1)
                dve.wait_ge(rope_in, h * 32 + 32)
                for pair in range(2):
                    n, e, b = h * 8 + pair * 4, base + 4 * pair, 4 * pair
                    cs, sn = (R3[:, 0:512], R3[:, 512:1024]), (R3[:, S:S + 512], R3[:, S + 512:S + 1024])
                    ac, as_, bs, bc = (t(0), t(2)), (t(1), r3(7)), (r3(4), r3(6)), (r3(5), r3(4))
                    dve.wait_ge(psum_full, e + 2)
                    TT(ac[0], bank(b), cs[0], ALU.mult)
                    TT(as_[0], bank(b), sn[0], ALU.mult).then_inc(psum_free, 1)
                    TT(ac[1], bank(b + 2), cs[1], ALU.mult)
                    TT(as_[1], bank(b + 2), sn[1], ALU.mult)
                    dve.wait_ge(psum_full, e + 4)
                    TT(bs[0], bank(b + 1), sn[0], ALU.mult)
                    TT(bc[0], bank(b + 1), cs[0], ALU.mult).then_inc(psum_free, 1)
                    TT(bs[1], bank(b + 3), sn[1], ALU.mult).then_inc(psum_free, 1)
                    dve.wait_ge(psum_free, e + 3)
                    TT(ac[0], ac[0], bs[0], ALU.subtract).then_inc(rope_out, 1)
                    dve.wait_ge(rope_out, n + 1)
                    TT(bc[1], bank(b + 3), cs[1], ALU.mult).then_inc(psum_free, 1)
                    TT(as_[0], bc[0], as_[0], ALU.add).then_inc(rope_out, 1)
                    TT(ac[1], ac[1], bs[1], ALU.subtract).then_inc(rope_out, 1)
                    dve.wait_ge(psum_free, e + 4)
                    TT(as_[1], bc[1], as_[1], ALU.add).then_inc(rope_out, 1)
                    for i in range(4):
                        hf, d = i // 2, i % 2
                        c = slice((2 * pair + d) * S + hf * 512, (2 * pair + d) * S + (hf + 1) * 512)
                        dve.wait_ge(qk_rounded, n + i + 1)
                        TT(a_lo[:, c], (as_ if d else ac)[hf], a_hi[:, c].bitcast(F32), ALU.subtract)\
                            .then_inc(qk_ready, 1)
                    dve.wait_ge(qk_ready, n + 4)
                for s in range(SB):
                    dve.wait_ge(g_sig, h * 8 + s + 1)
                    i = TT(r3(s), bank(J_G + s), t(s % 3), ALU.mult)
                    i.then_inc(psum_free, 1)
                dve.wait_ge(decay_in, h * 16 + 16)
                for i in range(len(SCORES) + 1):
                    if i < len(SCORES):
                        c, q, n = SCORES[i]
                        if i >= 3:
                            dve.wait_ge(s_ready, h * 16 + i - 2)
                        else:
                            dve.wait_ge(psum_free, base + J_S)
                        full(base + J_S + i)
                        dst, src, m = T[:, (i % 3) * 512:(i % 3) * 512 + n], bank(J_S + i, 0, n), q // P - c
                        if m == 0:
                            k = TT(dst, src, dk[:, 0:n], ALU.mult)
                        else:
                            k = STT(dst, src, dk[:, 511 + m:512 + m], dk[:, P:P + n], ALU.mult, ALU.mult)
                        k.then_inc(psum_free, 1)
                    if i:
                        n, a = SCORES[i - 1][2], SCORE_AT[i - 1]
                        dve.wait_ge(s_rounded, h * 16 + i)
                        TT(b_lo[:, a:a + n], T[:, ((i - 1) % 3) * 512:((i - 1) % 3) * 512 + n],
                           b_hi[:, a:a + n].bitcast(F32), ALU.subtract).then_inc(s_ready, 1)
                for s in range(SB):
                    dve.wait_ge(v_rounded, h * 8 + s + 1)
                    c = slice(s * 512, (s + 1) * 512)
                    i = TT(a_lo[:, c], bank(J_V + s), a_hi[:, c].bitcast(F32), ALU.subtract)
                    i.then_inc(psum_free, 1)
                for s in range(SB):
                    dve.wait_ge(o_sq, h * 8 + s + 1)
                    i = TT(r3(s), bank(J_O + s), r3(s), ALU.mult)
                    i.then_inc(psum_free, 1)
                TS(ssq[:], ssq[:], 1.0 / DV, EPS, ALU.mult, ALU.add).then_inc(o_var, 1)
                dve.wait_ge(psum_free, base + J_T)
                dve.wait_ge(o_root, h + 1)
                link(nc.vector.reciprocal(rstd[:], rstd[:]))
                for s in range(SB):
                    TS(r3(s), r3(s), rstd[:, s:s + 1], None, ALU.mult).then_inc(o_ready, 1)
                for s in range(SB):
                    dve.wait_ge(ot_rounded, h * 8 + s + 1)
                    cut = (slice(None), slice(None), slice(s * P, (s + 1) * P))
                    i = TT(b_lo[:, 0:4096].rearrange("p (d n) -> p d n", d=4)[cut],
                           bank(J_T + s).rearrange("p (d n) -> p d n", d=4),
                           b_hi[:, 0:4096].rearrange("p (d n) -> p d n", d=4)[cut].bitcast(F32), ALU.subtract)
                    i.then_inc(psum_free, 1)
                for nh in range(2):
                    for s in range(SB):
                        add(base + J_W + nh * 8 + s, J_W + nh * 8 + s, s, nh)
            step.end(HEADS)

            def ffn(layer):
                with dve.Fori(0, CHUNKS) as c:
                    base, n = JB_FFN[layer] + c * CHUNK_JOBS, (layer * CHUNKS + c) * 4
                    for tile in range(CT):
                        for hf in range(2):
                            i = tile * 2 + hf
                            dve.wait_ge(f_sig, n + i + 1)
                            k = TT(r3(4 + i), bank(4 * tile + 2 * hf), r3(i), ALU.mult)
                            k.then_inc(psum_free, 1)
                            dve.wait_ge(psum_free, base + 4 * tile + 2 * hf + 1)
                            full(base + 4 * tile + 2 + hf)
                            k = TT(r3(4 + i), r3(4 + i), bank(4 * tile + 2 * hf + 1), ALU.mult)
                            k.then_inc(psum_free, 1)
                        for i in (2 * tile, 2 * tile + 1):
                            dve.wait_ge(f_rounded, n + i + 1)
                            at = slice((i // 2) * S + (i % 2) * 512, (i // 2) * S + (i % 2) * 512 + 512)
                            TT(a_lo[:, at], r3(4 + i), a_hi[:, at].bitcast(F32), ALU.subtract)\
                                .then_inc(f_ready, 1)
                    for nh in range(2):
                        for s in range(SB):
                            add(base + 8 + nh * 8 + s, 8 + nh * 8 + s, s, nh)

            norm(1)
            ffn(0)
            norm(2)

            group_cols = cols[:, C_CONV:C_CONV + 96].rearrange("p (q c) -> p q c", q=8)

            def take(dst, g):
                return nc.vector.tensor_copy(dst[:].rearrange("p (q c) -> p q c", q=8),
                                             group_cols[:, :, bass.ds(GT * g, GT)])

            def conv(g, base, e0):
                link(take(gc_conv, g))
                for tile in range(GT):
                    full(base + e0 + 2 * tile + 1)
                    b = (e0 + 2 * tile) % 8 * BANK
                    u = uc[:, tile * S:(tile + 1) * S]

                    def w(j):
                        return gc_conv[:, 3 * j + tile:3 * j + tile + 1]

                    link(TS(u, ps[:, b:b + S], w(3), w(4), ALU.mult, ALU.add))
                    for back in (1, 2, 3):
                        i = STT(u[:, back:], ps[:, b:b + S - back], w(3 - back), u[:, back:], ALU.mult, ALU.add)
                        if back < 3:
                            link(i)
                    i.then_inc(psum_free, 2)

            def gelu_seen(g, e0):
                for tile in range(GT):
                    dve.wait_ge(gelu_done, 3 * g + tile + 1)
                    nc.vector.memset(small[:, 64 + tile:65 + tile], 0.0).then_inc(psum_free, 2)

            def u_split(g, u_hi, u_lo, tiles=range(GT)):
                for tile in tiles:
                    c = slice(tile * S, (tile + 1) * S)
                    dve.wait_ge(u_rounded, 3 * g + tile + 1)
                    TT(u_lo[:, c], uc[:, c], u_hi[:, c].bitcast(F32), ALU.subtract).then_inc(u_ready, 1)

            def gate_chain(g, y_hi, y_lo, meanwhile=None):
                def cut(i):
                    return slice(i % GT * S + i // GT * 512, i % GT * S + i // GT * 512 + 512)

                def gated(items):
                    for i in items:
                        dve.wait_ge(i_sig, 6 * g + i + 1)
                        TT(uc[:, cut(i)], uc[:, cut(i)], i_buf[i % 3], ALU.mult).then_inc(psum_free, 2)

                def scans(items):
                    first = step.now()
                    for j, i in enumerate(items):
                        dve.wait_ge(a_exp, 6 * g + i + 1)
                        dve.wait_ge(t_root, 6 * g + i + 1)
                        step.up(STT(s_buf[i % 2], r_buf[i % 4], 1.0, s_buf[i % 2], ALU.add, ALU.mult))
                    for j, i in enumerate(items):
                        dve.wait_ge(dve_step, first + j + 1)
                        step.up(TT(uc[:, cut(i)], uc[:, cut(i)], s_buf[i % 2], ALU.mult))
                    for j, i in enumerate(items):
                        dve.wait_ge(dve_step, first + j + 3)
                        tile, hf = i % GT, i // GT
                        start = uc[:, tile * S + 511:tile * S + 512] if hf else 0.0
                        k = nc.vector.tensor_tensor_scan(uc[:, cut(i)], r_buf[i % 4], uc[:, cut(i)], start,
                                                         ALU.mult, ALU.add)
                        k.then_inc(l_scan, 1)
                    for j, i in enumerate(items):
                        dve.wait_ge(l_scan, 6 * g + i + 1)
                        TT(R3[:, cut(i)], uc[:, cut(i)], R3[:, cut(i)], ALU.mult).then_inc(y_out, 1)

                def y_split(items):
                    for i in items:
                        dve.wait_ge(y_rounded, 6 * g + i + 1)
                        TT(y_lo[:, cut(i)], R3[:, cut(i)], y_hi[:, cut(i)].bitcast(F32), ALU.subtract)\
                            .then_inc(y_ready, 1)

                link(take(gc_gate, g))
                TS(gc_gate[:, 0:3], gc_gate[:, 21:24], -2.0, None, ALU.mult).then_inc(gc_ready, 1)
                gated((0, 1))
                scans((0, 1))
                gated((2, 3))
                y_split((0, 1))
                gated((4, 5))
                scans((2, 3))
                y_split((2, 3))
                if meanwhile is not None:
                    meanwhile()
                scans((4, 5))
                y_split((4, 5))

            per_turn = 1 + 3 * 3 + 1 + 6 * 2
            conv(0, JB_LRU, 0)
            u_split(0, a_hi, a_lo)
            gelu_seen(0, 6)
            gate_chain(0, a_hi, a_lo)
            with dve.Fori(1, GROUPS - 1) as g:
                base = JB_LRU + L_FIRST + (g - 1) * L_TURN
                step.n -= per_turn
                step.loop(g, per_turn)
                conv(g, base, 0)
                gelu_seen(g, 6)
                for s in range(SB):
                    add(base + L_OUT + s, L_OUT + s, s, 0)
                u_split(g, a_hi, a_lo, (0, 1))
                for s in range(SB):
                    add(base + L_OUT + 8 + s, L_OUT + 8 + s, s, 1)
                u_split(g, a_hi, a_lo, (2,))
                gate_chain(g, a_hi, a_lo)
            step.end(GROUPS - 1)

            base = JB_LRU + L_FIRST + (GROUPS - 2) * L_TURN
            conv(GROUPS - 1, base, 0)
            gelu_seen(GROUPS - 1, 6)
            u_split(GROUPS - 1, h_hi, h_lo)
            for s in range(SB):
                add(base + L_OUT + s, L_OUT + s, s, 0)

            def second_half_out():
                for s in range(SB):
                    add(base + L_RI_LAST + 12 + s, L_RI_LAST + 12 + s, s, 1)

            gate_chain(GROUPS - 1, h_hi, h_lo, second_half_out)
            for nh in range(2):
                for s in range(SB):
                    add(base + L_TURN + nh * 8 + s, nh * 8 + s, s, nh)
            norm(3)
            ffn(1)
            fn = scr[:, 0:D]
            for hf in range(2):
                q = slice(hf * 4, hf * 4 + 4)
                dve.wait_ge(n_sq, 8 * 4 + hf * 4 + 4)
                TS(ssq[:, q], ssq[:, q], 1.0 / D, EPS, ALU.mult, ALU.add).then_inc(n_var, 1)
                dve.wait_ge(n_root, 8 + hf + 1)
                link(nc.vector.reciprocal(rstd[:, q], rstd[:, q]))
                if hf == 0:
                    dve.wait_ge(fn_in, 16)
                for s in range(hf * 4, hf * 4 + 4):
                    STT(xn[:, s * D:(s + 1) * D], X[:, s * D:(s + 1) * D], rstd[:, s:s + 1], fn,
                        ALU.mult, ALU.mult).then_inc(out_ready, 1)


INS = ["x", "positions", "mix_norm", "ffn_norm", "final_norm", "ret_w_in", "ret_w_out", "lru_w_in",
       "lru_conv_w", "lru_conv_b", "lru_w_r", "lru_b_r", "lru_w_i", "lru_b_i", "lru_lambda", "lru_w_out",
       "ffn_w_gu", "ffn_w_down"]


def constants():
    import numpy as np
    freq = np.float32(10000.0) ** (-np.arange(P, dtype=np.float32) * np.float32(2.0) / np.float32(DK))
    log_gamma = np.log1p(-(2.0 ** (-5.0 - np.arange(HEADS, dtype=np.float64))))
    rel = np.arange(BANK, dtype=np.float64)[None, :] - np.arange(P, dtype=np.float64)[:, None]
    table = np.where(rel >= 0, np.exp(np.maximum(rel, 0.0) * log_gamma[:, None, None]), 0.0) * DK ** -0.5
    blocks = np.exp(P * np.arange(8)[None, None, :] * log_gamma[:, None, None]) * np.ones((1, P, 1))
    table = np.concatenate([table, blocks], axis=2)
    return {"inv_freq": freq.reshape(P, 1).astype(np.float32), "decay": table.astype(np.float32)}


def kernel(**inputs):
    import numpy as np
    import concourse.bacc as bacc
    from concourse.bass_utils import run_bass_kernel_spmd

    nc = bacc.Bacc("TRN2", target_bir_lowering=False, num_devices=1)
    arrays, args = {}, []
    given = {name: np.ascontiguousarray(inputs[name]) for name in INS}
    for name, a in {**given, **constants()}.items():
        arrays[f"in_{name}"] = a
        args.append(nc.dram_tensor(f"in_{name}", a.shape, mybir.dt.from_np(a.dtype), kind="ExternalInput").ap())
    y = nc.dram_tensor("out_y", (1, S, D), F32, kind="ExternalOutput").ap()
    build(nc, *args, y)
    r = run_bass_kernel_spmd(nc, [arrays], core_ids=[0])
    return r.results[0]["out_y"]
```

```python
from contextlib import ExitStack

import concourse.bass as bass
from concourse import mybir
from concourse.alu_op_type import AluOpType as ALU

ACT = mybir.ActivationFunctionType
AX_X = mybir.AxisListType.X
F32 = mybir.dt.float32
F32R = mybir.dt.float32r
I32 = mybir.dt.int32

P = 128
D = 1024
S = 1024
KT = D // P
SB = S // P
BANK = 512
EPS = 1e-6
HEADS = 4
DK = D // HEADS
DV = 2 * D // HEADS
LRU = 1536
BLOCK_W = LRU // 8
GT = 3
GROUPS = LRU // (GT * P)
FFN = 2816
CT = 2
CHUNKS = FFN // (CT * P)
RING = 3

SCORES = ([(c, P * c, BANK - P * c) for c in range(4)]
          + [(c, q, 256) for c in range(4) for q in (512, 768)]
          + [(c, P * c, S - P * c) for c in range(4, 8)])
SCORE_AT = [sum(n for _, _, n in SCORES[:i]) for i in range(len(SCORES))]
SCORE_COLS = sum(n for _, _, n in SCORES)
MEETS = [(0, 1), (0, 1, 2), (1, 2)]

J_QK, J_G, J_S, J_V, J_O, J_T, J_W = 0, 8, 16, 32, 40, 48, 56
HEAD_JOBS = 72
CHUNK_JOBS = 24
NORM_JOBS = 16
JB_NORM = [0]
JB_RET = NORM_JOBS
JB_NORM.append(JB_RET + HEADS * HEAD_JOBS)
JB_FFN = [JB_NORM[1] + NORM_JOBS]
JB_NORM.append(JB_FFN[0] + CHUNKS * CHUNK_JOBS)
JB_LRU = JB_NORM[2] + NORM_JOBS
L_FIRST, L_TURN, L_LAST = 24, 40, 16
JB_NORM.append(JB_LRU + L_FIRST + (GROUPS - 1) * L_TURN + L_LAST)
JB_FFN.append(JB_NORM[3] + NORM_JOBS)
JOBS = JB_FFN[1] + CHUNKS * CHUNK_JOBS
JB_NORM.append(JOBS)

L_OUT, L_RI, L_RI_LAST = 12, 28, 20

HEAD_UNITS, CHUNK_UNITS = 32, 12
UB_FFN = [HEADS * HEAD_UNITS]
UB_LRU = UB_FFN[0] + CHUNKS * CHUNK_UNITS
UB_FFN.append(UB_LRU + GROUPS * 18)
UNITS = UB_FFN[1] + CHUNKS * CHUNK_UNITS

FIRST, FIRST_LRU = (0, 2), (0, 1)

DVE_BLOCKS = 5
ACT_BLOCKS = SB - DVE_BLOCKS

C_MIX, C_FFN, C_CONV, C_CONVB, C_BR, C_BI, C_LAM = 0, 16, 32, 80, 92, 104, 116


class Tally:

    def __init__(self, sem):
        self.sem, self.base, self.n, self.turn, self.per = sem, 0, 0, None, 0

    def loop(self, turn, per):
        self.turn, self.per, self.start = turn, per, self.n

    def end(self, turns):
        assert self.n - self.start == self.per, (self.n - self.start, self.per)
        self.n = self.start + self.per * turns
        self.turn = None

    def up(self, ins):
        self.n += 1
        ins.then_inc(self.sem, 1)
        return ins

    def now(self):
        return self.n if self.turn is None else self.turn * self.per + self.n


def build(nc, x, positions, mix_norm, ffn_norm, final_norm, ret_w_in, ret_w_out, lru_w_in, lru_conv_w,
          lru_conv_b, lru_w_r, lru_b_r, lru_w_i, lru_b_i, lru_lambda, lru_w_out, ffn_w_gu, ffn_w_down,
          inv_freq, decay, out):
    ctx = ExitStack()
    with ctx:
        def sb(name, cols, dt=F32, stack=ctx):
            return stack.enter_context(nc.sbuf_tensor(name, [P, cols], dt))

        def sem(name):
            return ctx.enter_context(nc.semaphore(name))

        X = sb("residual", SB * D)
        h_hi, h_lo = sb("h_hi", KT * S, F32R), sb("h_lo", KT * S, F32R)
        raw = sb("w_raw", RING * 512)
        w_hi, w_lo = sb("w_hi", RING * 512, F32R), sb("w_lo", RING * 512, F32R)
        T = sb("tmp", 3 * 512)
        R3 = sb("gate_buf", 8 * 512)
        dk = sb("decay_sb", 520)
        ident = sb("ident", P)
        cols = sb("cols", P)
        gc_conv, gc_gate = sb("gc_conv", 24), sb("gc_gate", 24)
        ssq, rstd, invf, small = sb("ssq", 16), sb("rstd", 8), sb("invf", 1), sb("small", 72)
        eps = small[:, 70:71]
        with ExitStack() as one:
            xn = sb("xn", SB * D, F32, one)
        a_hi, a_lo = sb("a_hi", 4096, F32R), sb("a_lo", 4096, F32R)
        with ExitStack() as one:
            wri_hi, wri_lo = sb("wri_hi", 2304, F32R, one), sb("wri_lo", 2304, F32R, one)
            uc, wri_raw = sb("uc", 3072, F32, one), sb("wri_raw", 1152, F32, one)
        with ExitStack() as one:
            scr = sb("scratch", 9216, F32, one)
        with ExitStack() as one:
            pos = sb("pos", 1024, I32, one)
            turns_i = sb("turns_i", 1024, I32, one)
        b_hi, b_lo = sb("b_hi", SCORE_COLS, F32R), sb("b_lo", SCORE_COLS, F32R)
        assert SCORE_COLS == 4608
        ps = ctx.enter_context(nc.psum_tensor("ps", [P, 8 * BANK], F32))
        rope_dram = nc.dram_tensor("rope_tables", (2, P, S), F32, kind="Internal").ap()

        def bank(e, a=0, n=BANK):
            return ps[:, (e % 8) * BANK + a:(e % 8) * BANK + a + n]

        def nbank(n, i):
            b = [b for b in range(8) if b not in (FIRST_LRU if n == 2 else FIRST)][i % 6]
            return ps[:, b * BANK:(b + 1) * BANK]

        def last_out(i):
            c = slice(CT * S + i * 512, CT * S + (i + 1) * 512)
            return a_hi[:, c], a_lo[:, c]

        def norm_turns(n):
            if n == 0:
                return [(0, 4, 1), (4, SB, 2)]
            return [(0, SB, n + 2)] if n < 4 else [(s, s + 1, 6 + s) for s in range(SB)]

        def t(i):
            return T[:, i * 512:(i + 1) * 512]

        def r3(i, n=1):
            return R3[:, i * 512:(i + n) * 512]

        spare = [xn[:, c:c + 512] for c in (GT * S, GT * S + 512, 4096 + GT * S)]
        r_buf = (t(0), r3(6), dk[:, 0:512], spare[0])
        i_buf = (t(1), spare[1], spare[2])
        s_buf = (r3(7), t(2))

        x_in = [sem(f"x_in{i}") for i in range(SB)]
        vec_in, pos_in, fn_in = sem("vec_in"), sem("pos_in"), sem("fn_in")
        raw_in = [sem(f"raw_in{i}") for i in range(RING)]
        w_rounded, w_ready, w_begun = sem("w_rounded"), sem("w_ready"), sem("w_begun")
        ident_ready, vec_T, cols_ready = sem("ident_ready"), sem("vec_T"), sem("cols_ready")
        psum_full, psum_free = sem("psum_full"), sem("psum_free")
        dve_step, act_step = sem("dve_step"), sem("act_step")
        n_sq, n_sq_dve, n_var, n_root, n_rstd = (
            sem("n_sq"), sem("n_sq_dve"), sem("n_var"), sem("n_root"), sem("n_rstd"))
        xn_dve, xn_act, h_rounded = sem("xn_dve"), sem("xn_act"), sem("h_rounded")
        table_arg, rope_saved = sem("table_arg"), sem("rope_saved")
        rope_in, decay_in = sem("rope_in"), sem("decay_in")
        rope_out, qk_rounded, qk_ready = sem("rope_out"), sem("qk_rounded"), sem("qk_ready")
        s_rounded, s_ready = sem("s_rounded"), sem("s_ready")
        g_sig = sem("g_sig")
        v_rounded = sem("v_rounded")
        o_sq, o_var, o_root, o_ready = sem("o_sq"), sem("o_var"), sem("o_root"), sem("o_ready")
        ot_rounded = sem("ot_rounded")
        f_sig, f_rounded, f_ready = sem("f_sig"), sem("f_rounded"), sem("f_ready")
        lam_e, lam_sp = sem("lam_e"), sem("lam_sp")
        wri_in, wri_zero, wri_round, wri_ready = (
            sem("wri_in"), sem("wri_zero"), sem("wri_round"), sem("wri_ready"))
        u_rounded, u_ready = sem("u_rounded"), sem("u_ready")
        gelu_done, gc_ready = sem("gelu_done"), sem("gc_ready")
        r_sig, i_sig, r_tanh, a_exp, t_root = (
            sem("r_sig"), sem("i_sig"), sem("r_tanh"), sem("a_exp"), sem("t_root"))
        l_scan, y_out, y_rounded, y_ready = (
            sem("l_scan"), sem("y_out"), sem("y_rounded"), sem("y_ready"))
        out_ready, out_done = sem("out_ready"), sem("out_done")
        block = ctx.enter_context(nc.Block())

        @block.sync
        def _(sp):
            for s in range(SB):
                sp.dma_start(X[:, s * D:(s + 1) * D], x[0, s * P:(s + 1) * P, :]).then_inc(x_in[s], 16)
            vec = scr[:, 8 * 1024:8 * 1024 + P]
            for at, n, src in ((C_MIX, 16, mix_norm.rearrange("l (k p) -> (l k) p", p=P)),
                               (C_FFN, 16, ffn_norm.rearrange("l (k p) -> (l k) p", p=P)),
                               (C_CONV, 48, lru_conv_w[0].rearrange("j (k p) -> (j k) p", p=P)),
                               (C_CONVB, 12, lru_conv_b[0].rearrange("(k p) -> k p", p=P)),
                               (C_BR, 12, lru_b_r[0].rearrange("b c -> (b c)").rearrange("(k p) -> k p", p=P)),
                               (C_BI, 12, lru_b_i[0].rearrange("b c -> (b c)").rearrange("(k p) -> k p", p=P)),
                               (C_LAM, 12, lru_lambda[0].rearrange("(k p) -> k p", p=P))):
                sp.dma_start(vec[at:at + n, :], src).then_inc(vec_in, 16)
            sp.dma_start(pos[:], positions.to_broadcast([P, S])).then_inc(pos_in, 16)
            sp.dma_start(invf[:], inv_freq).then_inc(pos_in, 16)

            def load(slot, src, ready):
                if ready is not None:
                    sp.wait_ge(w_ready, ready)
                dst = raw[:, slot * 512:(slot + 1) * 512]
                if len(src.shape) == 3:
                    dst = dst.rearrange("p (k n) -> p k n", k=4)
                sp.dma_start(dst, src).then_inc(raw_in[slot], 16)

            def rows(w, kh, col):
                return w[kh * 512:(kh + 1) * 512, bass.ds(col, P)].rearrange("(k p) n -> p k n", p=P)

            def last(u, j, restart):
                return u - 1 if restart and j < 2 else u - 2

            def head(h, first):
                for j in range(HEAD_UNITS):
                    if j < 8:
                        tile, kh = j // 2, j % 2
                        src = rows(ret_w_in[0], kh, (tile // 2) * D + h * DK + (tile % 2) * P)
                    elif j < 24:
                        k = (j - 8) % 8
                        off = (2 * D + HEADS * DV) if j < 16 else 2 * D
                        src = ret_w_in[0][k * P:(k + 1) * P, bass.ds(off + h * DV, DV)]
                    else:
                        nh, k = (j - 24) // 4, (j - 24) % 4
                        src = ret_w_out[0][bass.ds(h * DV + k * P, P), nh * 512:(nh + 1) * 512]
                    load(j % RING, src, None if first and j < RING else
                         last(h * HEAD_UNITS + j, j, not first))
            head(0, True)
            with sp.Fori(1, HEADS) as h:
                head(h, False)

            def ffn(layer):
                def chunk(c, restart):
                    for j in range(CHUNK_UNITS):
                        if j < 8:
                            tile, up, kh = j // 4, (j // 2) % 2, j % 2
                            src = rows(ffn_w_gu[layer], kh, up * FFN + c * (CT * P) + tile * P)
                        else:
                            nh, k = (j - 8) // 2, j % 2
                            src = ffn_w_down[layer][bass.ds(c * (CT * P) + k * P, P), nh * 512:(nh + 1) * 512]
                        load(j % RING, src, last(UB_FFN[layer] + c * CHUNK_UNITS + j, j, restart))
                chunk(0, layer == 0)
                with sp.Fori(1, CHUNKS) as c:
                    chunk(c, False)

            ffn(0)

            def gates(g, w, n, behind=None):
                sp.wait_ge(wri_ready, n)
                sp.wait_ge(wri_zero, 1)
                a = w[0][bass.ds(2 * g, 1)].rearrange("a c d -> (a c) d")
                b = w[0][bass.ds(2 * g + 1, 1)].rearrange("a c d -> (a c) d")
                r = wri_raw
                pieces = ((r[:, 0:192], a[0:128, :]), (r[0:64, 384:576], a[128:192, :]),
                          (r[64:128, 576:768], b[0:64, :]), (r[:, 960:1152], b[64:192, :]))
                for dst, src in pieces:
                    if behind is not None and dst is pieces[-1][0]:
                        sp.wait_ge(w_ready, behind)
                    sp.dma_start(dst, src).then_inc(wri_in, 16)

            def into(g, gate, u0, waited=False):
                for j in range(6):
                    tile, kh = j // 2, j % 2
                    src = rows(lru_w_in[0], kh, (0 if gate else LRU) + g * (GT * P) + tile * P)
                    load(j % RING, src, None if waited and j == 0 else last(u0 + j, j, False))

            def outof(g, u0):
                for j in range(6):
                    nh, k = j // 3, j % 3
                    src = lru_w_out[0][bass.ds(g * (GT * P) + k * P, P), nh * 512:(nh + 1) * 512]
                    load(j % RING, src, last(u0 + j, j, False))

            into(0, False, UB_LRU)
            gates(0, lru_w_r, 0)
            into(0, True, UB_LRU + 6)
            gates(0, lru_w_i, 1)
            with sp.Fori(1, GROUPS) as g:
                u0 = UB_LRU + g * 18 - 6
                into(g, False, u0)
                gates(g, lru_w_r, 2 * g, last(u0 + 6, 0, False))
                into(g, True, u0 + 6, waited=True)
                gates(g, lru_w_i, 2 * g + 1)
                outof(g - 1, u0 + 12)
            outof(GROUPS - 1, UB_LRU + GROUPS * 18 - 6)
            ffn(1)
            sp.wait_ge(psum_free, JB_NORM[3])
            sp.dma_start(scr[:, 0:D], final_norm.rearrange("(a n) -> a n", a=1).to_broadcast([P, D]))\
              .then_inc(fn_in, 16)
            for s in range(SB):
                sp.wait_ge(out_ready, s + 1)
                sp.dma_start(out[0, s * P:(s + 1) * P, :], X[:, s * D:(s + 1) * D]).then_inc(out_done, 16)
            sp.wait_ge(out_done, 16 * SB)

        @block.gpsimd
        def _(pool):
            nc.gpsimd.memset(ident[:], 0.0).then_inc(ident_ready, 1)
            pool.wait_ge(ident_ready, 1)
            nc.gpsimd.affine_select(out=ident[:], in_=ident[:], compare_op=ALU.not_equal, fill=1.0, base=0,
                                    pattern=[[-1, P]], channel_multiplier=1).then_inc(ident_ready, 1)

            def touch(col):
                nc.gpsimd.tensor_tensor(small[:, 62:63], col, col, ALU.subtract)

            def split(slot, loads, u, used, place=None):
                cut = slice(slot * 512, (slot + 1) * 512)
                hi, lo = (w_hi[:, cut], w_lo[:, cut]) if place is None else place
                pool.wait_ge(raw_in[slot], loads)
                if used is not None:
                    pool.wait_ge(w_begun, used)
                touch(raw[:, slot * 512:slot * 512 + 1])
                nc.gpsimd.tensor_copy(hi, raw[:, cut]).then_inc(w_rounded, 1)
                pool.wait_ge(w_rounded, u + 1)
                nc.gpsimd.tensor_tensor(lo, raw[:, cut], hi.bitcast(F32), ALU.subtract).then_inc(w_ready, 1)

            def head(h, first):
                for j in range(HEAD_UNITS):
                    u, slot = h * HEAD_UNITS + j, j % RING
                    used = None if first and j < RING else u if j < 2 else u - 1
                    split(slot, 16 * (h * (11 if slot < 2 else 10) + j // RING + 1), u, used)
            head(0, True)
            with pool.Fori(1, HEADS) as h:
                head(h, False)
            landed = [HEADS * (11 if slot < 2 else 10) for slot in range(RING)]

            def units(n, u0, before, restart=False):
                for j in range(n):
                    split(j % RING, 16 * (before[j % RING] + j // RING + 1), u0 + j,
                          u0 + j - (0 if restart and j < 2 else 1))

            def ffn(layer, landed):
                def chunk(c, restart):
                    units(CHUNK_UNITS, UB_FFN[layer] + c * CHUNK_UNITS, [c * 4 + n for n in landed], restart)
                chunk(0, layer == 0)
                with pool.Fori(1, CHUNKS - layer) as c:
                    chunk(c, False)
                if layer == 1:
                    u0, before = UB_FFN[1] + (CHUNKS - 1) * CHUNK_UNITS, [(CHUNKS - 1) * 4 + n for n in landed]
                    units(8, u0, before)
                    for j in range(8, CHUNK_UNITS):
                        split(j % RING, 16 * (before[j % RING] + j // RING + 1), u0 + j, None, last_out(j - 8))

            ffn(0, landed)
            landed = [n + 4 * CHUNKS for n in landed]
            pool.wait_ge(psum_full, JB_NORM[2])
            nc.gpsimd.memset(wri_raw[:], 0.0).then_inc(wri_zero, 1)

            def gates(g, n, at):
                pool.wait_ge(wri_in, 64 * (n + 1))
                touch(wri_raw[:, 0:1])
                cut = slice(at * 1152, (at + 1) * 1152)
                nc.gpsimd.tensor_copy(wri_hi[:, cut], wri_raw[:]).then_inc(wri_round, 1)
                pool.wait_ge(wri_round, n + 1)
                nc.gpsimd.tensor_tensor(wri_lo[:, cut], wri_raw[:], wri_hi[:, cut].bitcast(F32),
                                        ALU.subtract).then_inc(wri_ready, 1)

            units(6, UB_LRU, landed)
            gates(0, 0, 0)
            units(6, UB_LRU + 6, [n + 2 for n in landed])
            gates(0, 1, 1)
            with pool.Fori(1, GROUPS) as g:
                u0 = UB_LRU + g * 18 - 6
                now = [n + g * 6 - 2 for n in landed]
                units(6, u0, now)
                pool.wait_ge(psum_full, JB_LRU + L_FIRST + (g - 1) * L_TURN + 1)
                gates(g, 2 * g, 0)
                units(6, u0 + 6, [n + 2 for n in now])
                gates(g, 2 * g + 1, 1)
                units(6, u0 + 12, [n + 4 for n in now])
            units(6, UB_LRU + GROUPS * 18 - 6, [n + GROUPS * 6 - 2 for n in landed])
            ffn(1, [n + GROUPS * 6 for n in landed])

        @block.tensor
        def _(pe):
            def free(e):
                pe.wait_ge(psum_free, e - 7)

            def three(o, l_hi, l_lo, r_hi, r_lo, start, stop, begins=False):
                m = nc.tensor.matmul(o, l_hi, r_hi, start=start, stop=False)
                if begins:
                    m.then_inc(w_begun, 1)
                nc.tensor.matmul(o, l_hi, r_lo, start=False, stop=False)
                return nc.tensor.matmul(o, l_lo, r_hi, start=False, stop=stop)

            def rows_unit(j, u, kh, banks):
                pe.wait_ge(w_ready, u + 1)
                for kk in range(4):
                    w = slice((j % RING) * 512 + kk * P, (j % RING) * 512 + (kk + 1) * P)
                    for hf in range(2):
                        r = slice((kh * 4 + kk) * S + hf * 512, (kh * 4 + kk) * S + (hf + 1) * 512)
                        m = three(bank(banks[hf]), w_hi[:, w], w_lo[:, w], h_hi[:, r], h_lo[:, r],
                                  kh == 0 and kk == 0, kh == 1 and kk == 3, kk == 0 and hf == 0)
                        if kh == 1 and kk == 3:
                            m.then_inc(psum_full, 1)

            def cols_unit(j, u, k, nk, l_hi, l_lo, at, e0, base, ready=None):
                pe.wait_ge(w_ready, u + 1)
                w = slice((j % RING) * 512, (j % RING + 1) * 512)
                for s in range(SB):
                    if k == 0:
                        free(base + e0 + s)
                    if ready is not None:
                        pe.wait_ge(ready[0], ready[1](s))
                    c = at + s * P
                    m = three(bank(e0 + s), l_hi[:, c:c + P], l_lo[:, c:c + P], w_hi[:, w], w_lo[:, w],
                              k == 0, k == nk - 1, s == 0)
                    if k == nk - 1:
                        m.then_inc(psum_full, 1)

            def tile_rows(j, u, base, banks, wait):
                free(base + wait)
                rows_unit(j, u, 0, banks)
                rows_unit(j + 1, u + 1, 1, banks)

            def norm_and_tile(n, u0, banks):
                e0 = JB_NORM[n]

                def transposes(k):
                    for hf in range(2):
                        i = 2 * k + hf
                        if n == 0 and i == 0:
                            pe.wait_ge(ident_ready, 2)
                        elif i == 0:
                            pe.wait_ge(psum_free, e0)
                        if i >= 6:
                            pe.wait_ge(psum_free, e0 + i - 5)
                        for s in range(4):
                            block, half = hf * 4 + s, 2 * n + k // 4
                            if k in (0, 4):
                                if block < DVE_BLOCKS:
                                    pe.wait_ge(xn_dve, half * DVE_BLOCKS + block + 1)
                                else:
                                    pe.wait_ge(xn_act, half * ACT_BLOCKS + block - DVE_BLOCKS + 1)
                            c = block * D + k * P
                            m = nc.tensor.transpose(nbank(n, i)[:, s * P:(s + 1) * P], xn[:, c:c + P], ident[:])
                        m.then_inc(psum_full, 1)

                def products(k):
                    pe.wait_ge(psum_free, e0 + 2 * k + 2)
                    if k % 4 == 0:
                        pe.wait_ge(w_ready, u0 + k // 4 + 1)
                    w = slice(k * P, (k + 1) * P)
                    for hf in range(2):
                        r = slice(k * S + hf * 512, k * S + (hf + 1) * 512)
                        m = three(bank(banks[hf]), w_hi[:, w], w_lo[:, w], h_hi[:, r], h_lo[:, r],
                                  k == 0, k == KT - 1, k % 4 == 0 and hf == 0)
                        if k == KT - 1:
                            m.then_inc(psum_full, 1)

                for k in range(KT + 2):
                    if k < KT:
                        transposes(k)
                    if n == 0 and k == 0:
                        pe.wait_ge(vec_in, 16 * 7)
                        nc.tensor.transpose(ps[:, 0:P], scr[:, 8 * 1024:8 * 1024 + P], ident[:])\
                          .then_inc(vec_T, 1)
                    if k >= 2:
                        products(k - 2)

            def head(h, first):
                base, ub = JB_RET + h * HEAD_JOBS, h * HEAD_UNITS
                for tile in range(4):
                    b = 4 * (tile // 2) + tile % 2
                    if first and tile == 0:
                        norm_and_tile(0, ub, FIRST)
                    else:
                        tile_rows(2 * tile, ub + 2 * tile, base, (b, b + 2), b + 2)
                for k in range(KT):
                    cols_unit(8 + k, ub + 8 + k, k, KT, h_hi, h_lo, k * S, J_G, base)
                for i, (c, q, n) in enumerate(SCORES):
                    if i == 0:
                        pe.wait_ge(qk_ready, h * 8 + 8)
                    free(base + J_S + i)
                    for d in range(2):
                        kc, qc = (2 + d) * S + c * P, d * S + q
                        m = three(bank(J_S + i, 0, n), a_hi[:, kc:kc + P], a_lo[:, kc:kc + P],
                                  a_hi[:, qc:qc + n], a_lo[:, qc:qc + n], d == 0, d == 1)
                    m.then_inc(psum_full, 1)
                for k in range(KT):
                    cols_unit(16 + k, ub + 16 + k, k, KT, h_hi, h_lo, k * S, J_V, base)
                pe.wait_ge(s_ready, h * 16 + 16)
                for s in range(SB):
                    free(base + J_O + s)
                    pe.wait_ge(psum_free, base + J_V + s + 1)
                    for c in range(s + 1):
                        i = next(i for i, (cc, q, n) in enumerate(SCORES) if cc == c and q <= s * P < q + n)
                        a = SCORE_AT[i] + s * P - SCORES[i][1]
                        m = three(bank(J_O + s), b_hi[:, a:a + P], b_lo[:, a:a + P],
                                  a_hi[:, c * 512:(c + 1) * 512], a_lo[:, c * 512:(c + 1) * 512],
                                  c == 0, c == s)
                    m.then_inc(psum_full, 1)
                for s in range(SB):
                    free(base + J_T + s)
                    pe.wait_ge(o_ready, h * 8 + s + 1)
                    for d in range(4):
                        m = nc.tensor.transpose(bank(J_T + s, d * P, P),
                                                R3[:, s * 512 + d * P:s * 512 + (d + 1) * P], ident[:])
                    m.then_inc(psum_full, 1)
                for nh in range(2):
                    for k in range(4):
                        j = 24 + nh * 4 + k
                        cols_unit(j, ub + j, k, 4, b_hi, b_lo, k * S, J_W + nh * 8, base,
                                  (psum_free, lambda s: base + J_T + s + 1) if nh == 0 and k == 0 else None)

            head(0, True)
            with pe.Fori(1, HEADS) as h:
                head(h, False)

            def ffn(layer):
                def chunk(c, first=False, last=False):
                    base, ub = JB_FFN[layer] + c * CHUNK_JOBS, UB_FFN[layer] + c * CHUNK_UNITS
                    for i in range(4):
                        b = 4 * (i // 2) + i % 2
                        if first and i == 0:
                            norm_and_tile(2 * layer + 1, ub, FIRST)
                        else:
                            tile_rows(2 * i, ub + 2 * i, base, (b, b + 2), b + 2)
                    if last:
                        def part(s, nh, k):
                            if s == 0:
                                pe.wait_ge(w_ready, ub + 8 + 2 * nh + k + 1)
                            if s == 0 and nh == 0:
                                pe.wait_ge(f_ready, (layer * CHUNKS + c) * 4 + 2 * k + 2)
                            e, at, w = 8 + 2 * s + nh, k * S + s * P, last_out(2 * nh + k)
                            if k == 0:
                                free(base + e)
                            m = three(bank(e), a_hi[:, at:at + P], a_lo[:, at:at + P], w[0], w[1],
                                      k == 0, k == CT - 1)
                            if k == CT - 1:
                                m.then_inc(psum_full, 1)

                        for k in range(CT):
                            for s in range(4):
                                for nh in range(2):
                                    part(s, nh, k)
                        for s in range(4, SB):
                            for nh in range(2):
                                for k in range(CT):
                                    part(s, nh, k)
                        return
                    for nh in range(2):
                        for k in range(CT):
                            if nh == 0:
                                pe.wait_ge(f_ready, (layer * CHUNKS + c) * 4 + 2 * k + 2)
                            j = 8 + nh * 2 + k
                            cols_unit(j, ub + j, k, CT, a_hi, a_lo, k * S, 8 + nh * 8, base)
                chunk(0, first=True)
                with pe.Fori(1, CHUNKS - layer) as c:
                    chunk(c)
                if layer == 1:
                    chunk(CHUNKS - 1, last=True)

            ffn(0)

            def lru_into(u0, base, e0, first=False):
                for tile in range(GT):
                    e = e0 + 2 * tile
                    if first and tile == 0:
                        norm_and_tile(2, u0, FIRST_LRU)
                    else:
                        tile_rows(2 * tile, u0 + 2 * tile, base, (e, e + 1), e + 1)

            def lru_gates(g, base, e0, u_hi, u_lo):
                pe.wait_ge(wri_ready, 2 * g + 2)
                for hf in range(2):
                    for tile in range(GT):
                        for m_i in range(2):
                            e = e0 + (hf * GT + tile) * 2 + m_i
                            free(base + e)
                            if hf == 0 and m_i == 0 and tile < 2:
                                pe.wait_ge(u_ready, 3 * g + 2 + tile)
                            for kt in MEETS[tile]:
                                w = slice(m_i * 1152 + kt * 384 + tile * P, m_i * 1152 + kt * 384 + (tile + 1) * P)
                                r = slice(kt * S + hf * 512, kt * S + (hf + 1) * 512)
                                m = three(bank(e), wri_hi[:, w], wri_lo[:, w], u_hi[:, r], u_lo[:, r],
                                          kt == MEETS[tile][0], kt == MEETS[tile][-1])
                            m.then_inc(psum_full, 1)

            def lru_outof(g, u0, base, e0, nh, y_hi, y_lo):
                for k in range(GT):
                    j = nh * 3 + k
                    if nh == 0:
                        pe.wait_ge(y_ready, g * 6 + k + 4)
                    cols_unit(j, u0 + j, k, GT, y_hi, y_lo, k * S, e0, base)

            lru_into(UB_LRU, JB_LRU, 0, True)
            lru_into(UB_LRU + 6, JB_LRU, 6)
            lru_gates(0, JB_LRU, 12, a_hi, a_lo)
            with pe.Fori(1, GROUPS - 1) as g:
                base, u0 = JB_LRU + L_FIRST + (g - 1) * L_TURN, UB_LRU + g * 18 - 6
                lru_into(u0, base, 0)
                lru_into(u0 + 6, base, 6)
                for nh in range(2):
                    lru_outof(g - 1, u0 + 12, base, L_OUT + 8 * nh, nh, a_hi, a_lo)
                lru_gates(g, base, L_RI, a_hi, a_lo)
            base, u0 = JB_LRU + L_FIRST + (GROUPS - 2) * L_TURN, UB_LRU + (GROUPS - 1) * 18 - 6
            lru_into(u0, base, 0)
            lru_into(u0 + 6, base, 6)
            lru_outof(GROUPS - 2, u0 + 12, base, L_OUT, 0, a_hi, a_lo)
            lru_gates(GROUPS - 1, base, L_RI_LAST, h_hi, h_lo)
            lru_outof(GROUPS - 2, u0 + 12, base, L_RI_LAST + 12, 1, a_hi, a_lo)
            for nh in range(2):
                lru_outof(GROUPS - 1, u0 + 18, base + L_TURN, 8 * nh, nh, h_hi, h_lo)
            ffn(1)

        @block.scalar
        def _(act):
            def full(e):
                act.wait_ge(psum_full, e + 1)

            def square_rows(s, half):
                c = s * D + half * 512
                nc.scalar.activation(R3[:, s * 512:(s + 1) * 512], X[:, c:c + 512], ACT.Square,
                                     accum_out=ssq[:, half * 8 + s:half * 8 + s + 1]).then_inc(n_sq, 1)

            def load_sqrt():
                nc.scalar.activation(small[:, 71:72], ident[:, 0:1], ACT.Sqrt)

            def stats(n):
                if n:
                    load_sqrt()
                    for s in range(SB):
                        act.wait_ge(psum_free, JB_NORM[n] - 15 + s)
                        square_rows(s, 0)
                for first, end, turn in norm_turns(n):
                    for s in range(first, end):
                        if n == 0:
                            act.wait_ge(x_in[s], 16)
                            square_rows(s, 0)
                        else:
                            act.wait_ge(psum_free, JB_NORM[n] - 7 + s)
                            act.wait_ge(n_sq, 16 * n - 8 + s + 1)
                            square_rows(s, 1)
                    act.wait_ge(n_var, turn)
                    nc.scalar.activation(rstd[:, first:end], ssq[:, first:end],
                                         ACT.Sqrt, bias=eps, scale=1.0 / D).then_inc(n_root, 1)

            def norm(n):
                stats(n)

                def scaled(half):
                    for s in range(DVE_BLOCKS, SB):
                        c = s * D + half * 512
                        nc.scalar.activation(xn[:, c:c + 512], X[:, c:c + 512], ACT.Copy,
                                             scale=rstd[:, s:s + 1]).then_inc(xn_act, 1)

                act.wait_ge(n_rstd, n + 2)
                scaled(0)
                if n == 0:
                    act.wait_ge(cols_ready, 1)
                for k in range(KT):
                    for hf in range(2):
                        i = 2 * k + hf
                        full(JB_NORM[n] + i)
                        g = (C_MIX + (n // 2) * 8 if n % 2 == 0 else C_FFN + (n // 2) * 8) + k
                        nc.scalar.activation(h_hi[:, k * S + hf * 512:k * S + (hf + 1) * 512], nbank(n, i),
                                             ACT.Copy, scale=cols[:, g:g + 1]).then_inc(h_rounded, 1)
                    if k == 0:
                        scaled(1)

            norm(0)
            for i in range(2):
                act.wait_ge(table_arg, i + 1)
                if i == 0:
                    act.wait_ge(n_sq, 8)
                nc.scalar.activation(R3[:, (1 - i) * S:(2 - i) * S], scr[:, (2 + i) * S:(3 + i) * S],
                                     ACT.Sin).then_inc(rope_in, 16)
                act.wait_ge(rope_in, 16 * (i + 1))
                act.dma_start(rope_dram[i], R3[:, (1 - i) * S:(2 - i) * S]).then_inc(rope_saved, 16)

            def head(h, first):
                base = JB_RET + h * HEAD_JOBS
                if not first:
                    act.wait_ge(psum_full, base)
                    act.dma_start(R3[:, 0:S], rope_dram[1]).then_inc(rope_in, 16)
                    act.dma_start(R3[:, S:2 * S], rope_dram[0]).then_inc(rope_in, 16)
                act.dma_start(dk[:], decay[bass.ds(h, 1)].rearrange("a p n -> (a p) n")).then_inc(decay_in, 16)
                for i in range(8):
                    pair, hf, d = i // 4, (i // 2) % 2, i % 2
                    act.wait_ge(rope_out, h * 8 + i + 1)
                    c = (2 * pair + d) * S + hf * 512
                    nc.scalar.activation(a_hi[:, c:c + 512], (t(0), t(1), t(2), r3(7))[i % 4], ACT.Copy)\
                        .then_inc(qk_rounded, 1)
                for s in range(SB):
                    full(base + J_G + s)
                    if s == 0:
                        act.wait_ge(qk_ready, h * 8 + 8)
                    if s >= 3:
                        act.wait_ge(psum_free, base + J_G + s - 2)
                    nc.scalar.activation(t(s % 3), bank(J_G + s), ACT.Sigmoid).then_inc(g_sig, 1)
                for i, (c, q, n) in enumerate(SCORES):
                    act.wait_ge(psum_free, base + J_S + i + 1)
                    nc.scalar.activation(b_hi[:, SCORE_AT[i]:SCORE_AT[i] + n], T[:, (i % 3) * 512:(i % 3) * 512 + n],
                                         ACT.Copy).then_inc(s_rounded, 1)
                for s in range(SB):
                    full(base + J_V + s)
                    nc.scalar.activation(a_hi[:, s * 512:(s + 1) * 512], bank(J_V + s), ACT.Copy)\
                        .then_inc(v_rounded, 1)
                act.wait_ge(s_ready, h * 16 + 16)
                load_sqrt()
                for s in range(SB):
                    full(base + J_O + s)
                    if s >= 3:
                        act.wait_ge(o_sq, h * 8 + s - 2)
                    nc.scalar.activation(t(s % 3), bank(J_O + s), ACT.Square,
                                         accum_out=ssq[:, s:s + 1]).then_inc(o_sq, 1)
                    if s % 4 == 3:
                        act.wait_ge(o_var, 2 * h + s // 4 + 1)
                        nc.scalar.activation(rstd[:, s - 3:s + 1], ssq[:, s - 3:s + 1], ACT.Sqrt)\
                            .then_inc(o_root, 1)
                for s in range(SB):
                    full(base + J_T + s)
                    nc.scalar.activation(b_hi[:, 0:4096].rearrange("p (d n) -> p d n", d=4)[:, :, s * P:(s + 1) * P],
                                         bank(J_T + s).rearrange("p (d n) -> p d n", d=4), ACT.Copy)\
                        .then_inc(ot_rounded, 1)

            head(0, True)
            act.wait_ge(rope_saved, 32)
            with act.Fori(1, HEADS) as h:
                head(h, False)

            def ffn(layer):
                with act.Fori(0, CHUNKS) as c:
                    base, n = JB_FFN[layer] + c * CHUNK_JOBS, (layer * CHUNKS + c) * 4

                    def rounded(i):
                        act.wait_ge(psum_free, base + 2 * i + 2)
                        at = (i // 2) * S + (i % 2) * 512
                        nc.scalar.activation(a_hi[:, at:at + 512], r3(4 + i), ACT.Copy).then_inc(f_rounded, 1)

                    for tile in range(CT):
                        for hf in range(2):
                            i = tile * 2 + hf
                            act.wait_ge(psum_full, base + 4 * tile + hf + 1)
                            nc.scalar.activation(r3(i), bank(4 * tile + 2 * hf), ACT.Sigmoid).then_inc(f_sig, 1)
                        rounded(2 * tile)
                        rounded(2 * tile + 1)

            norm(1)
            act.wait_ge(lam_e, 1)
            nc.scalar.activation(small[:, 12:24], small[:, 0:12], ACT.Exp).then_inc(lam_sp, 1)
            ffn(0)
            norm(2)

            def gelu(g, base, e0):
                for tile in range(GT):
                    full(base + e0 + 2 * tile + 1)
                    act.wait_ge(y_ready, g * 6)
                    b = (e0 + 2 * tile) % 8 * BANK
                    nc.scalar.activation(R3[:, tile * S:(tile + 1) * S], ps[:, b:b + 2 * BANK],
                                         ACT.Gelu_apprx_tanh).then_inc(gelu_done, 1)

            def u_round(g, base, u_hi, begun=None, full_to=None):
                for tile in range(GT):
                    if begun is not None and tile < 2:
                        act.wait_ge(w_begun, begun + tile)
                    elif full_to is not None:
                        act.wait_ge(psum_full, full_to)
                    act.wait_ge(psum_free, base + 2 * tile + 2)
                    nc.scalar.activation(u_hi[:, tile * S:(tile + 1) * S], uc[:, tile * S:(tile + 1) * S],
                                         ACT.Copy).then_inc(u_rounded, 1)

            def gate_chain(g, base, e0, y_hi):
                def gates(i):
                    tile = i % GT
                    if i >= 4:
                        act.wait_ge(l_scan, 6 * g + i - 3)
                    full(base + e0 + 2 * i)
                    nc.scalar.activation(r_buf[i % 4], bank(e0 + 2 * i), ACT.Sigmoid,
                                         bias=gc_gate[:, 15 + tile:16 + tile]).then_inc(r_sig, 1)
                    full(base + e0 + 2 * i + 1)
                    if i >= 3:
                        act.wait_ge(psum_free, base + e0 + 2 * i - 4)
                    nc.scalar.activation(i_buf[i % 3], bank(e0 + 2 * i + 1), ACT.Sigmoid,
                                         bias=gc_gate[:, 18 + tile:19 + tile]).then_inc(i_sig, 1)

                def tanh_exp(items):
                    for i in items:
                        if i >= 2:
                            act.wait_ge(l_scan, 6 * g + i - 1)
                        act.wait_ge(r_sig, 6 * g + i + 1)
                        nc.scalar.activation(s_buf[i % 2], r_buf[i % 4], ACT.Tanh,
                                             scale=gc_gate[:, 21 + i % GT:22 + i % GT]).then_inc(r_tanh, 1)
                    for i in items:
                        act.wait_ge(r_tanh, 6 * g + i + 1)
                        nc.scalar.activation(r_buf[i % 4], r_buf[i % 4], ACT.Exp,
                                             scale=gc_gate[:, i % GT:i % GT + 1]).then_inc(a_exp, 1)

                def roots(items):
                    for i in items:
                        nc.scalar.activation(s_buf[i % 2], s_buf[i % 2], ACT.Sqrt).then_inc(t_root, 1)

                def y_round(items):
                    for i in items:
                        act.wait_ge(y_out, 6 * g + i + 1)
                        act.wait_ge(psum_full, base + e0 + (6 if i < GT else 12))
                        at = i % GT * S + i // GT * 512
                        nc.scalar.activation(y_hi[:, at:at + 512], R3[:, at:at + 512], ACT.Copy)\
                            .then_inc(y_rounded, 1)

                act.wait_ge(gc_ready, g + 1)
                gates(0)
                gates(1)
                tanh_exp((0, 1))
                roots((0, 1))
                gates(2)
                gates(3)
                y_round((0, 1))
                gates(4)
                gates(5)
                tanh_exp((2, 3))
                roots((2, 3))
                tanh_exp((4, 5))
                y_round((2, 3))
                roots((4, 5))
                y_round((4, 5))

            u_round(0, JB_LRU, a_hi)
            gelu(0, JB_LRU, 6)
            gate_chain(0, JB_LRU, 12, a_hi)
            with act.Fori(1, GROUPS - 1) as g:
                base = JB_LRU + L_FIRST + (g - 1) * L_TURN
                gelu(g, base, 6)
                u_round(g, base, a_hi, UB_LRU + g * 18 - 6 + 12 + GT + 2, base + L_RI)
                gate_chain(g, base, L_RI, a_hi)
            base = JB_LRU + L_FIRST + (GROUPS - 2) * L_TURN
            gelu(GROUPS - 1, base, 6)
            u_round(GROUPS - 1, base, h_hi, None, base + L_OUT)
            gate_chain(GROUPS - 1, base, L_RI_LAST, h_hi)
            norm(3)
            ffn(1)
            load_sqrt()
            for s, _, turn in norm_turns(4):
                act.wait_ge(psum_free, JOBS - 14 + 2 * s)
                if s >= 4:
                    act.wait_ge(n_sq, 56 + s - 3)
                nc.scalar.activation(R3[:, s % 4 * D:(s % 4 + 1) * D], X[:, s * D:(s + 1) * D], ACT.Square,
                                     accum_out=ssq[:, s:s + 1]).then_inc(n_sq, 1)
                act.wait_ge(n_sq, 56 + s + 1)
                nc.scalar.activation(rstd[:, s:s + 1], ssq[:, s:s + 1], ACT.Sqrt, bias=eps, scale=1.0 / D)\
                    .then_inc(n_root, 1)

        @block.vector
        def _(dve):
            step = Tally(dve_step)

            def link(ins):
                step.up(ins)
                dve.wait_ge(dve_step, step.now())

            def full(e):
                dve.wait_ge(psum_full, e + 1)

            TT, TS, STT = nc.vector.tensor_tensor, nc.vector.tensor_scalar, nc.vector.scalar_tensor_tensor

            def inverse_root(n, first=0, end=SB, turn=None):
                turn = n + 2 if turn is None else turn
                if n == 0:
                    for s in range(first, end):
                        dve.wait_ge(x_in[s], 16)
                        c = s * D + 512
                        STT(scr[:, 2048 + s * 512:2048 + (s + 1) * 512], X[:, c:c + 512], 1.0, X[:, c:c + 512],
                            ALU.mult, ALU.mult, accum_out=ssq[:, 8 + s:9 + s]).then_inc(n_sq_dve, 1)
                    dve.wait_ge(n_sq_dve, end)
                dve.wait_ge(n_sq, 16 * n + end)
                TT(ssq[:, first:end], ssq[:, first:end], ssq[:, 8 + first:8 + end], ALU.add).then_inc(n_var, 1)
                dve.wait_ge(n_root, turn)
                nc.vector.reciprocal(rstd[:, first:end], rstd[:, first:end]).then_inc(n_rstd, 1)
                dve.wait_ge(n_rstd, turn)

            def norm(n):
                def scaled(half, first=0, end=DVE_BLOCKS):
                    for s in range(first, min(end, DVE_BLOCKS)):
                        c = s * D + half * 512
                        TS(xn[:, c:c + 512], X[:, c:c + 512], rstd[:, s:s + 1], None, ALU.mult)\
                            .then_inc(xn_dve, 1)

                for first, end, turn in norm_turns(n):
                    inverse_root(n, first, end, turn)
                    scaled(0, first, end)
                if n == 0:
                    dve.wait_ge(vec_T, 1)
                    nc.vector.tensor_copy(cols[:], ps[:, 0:P]).then_inc(cols_ready, 1)
                for k in range(KT):
                    for hf in range(2):
                        i = 2 * k + hf
                        g = (C_MIX + (n // 2) * 8 if n % 2 == 0 else C_FFN + (n // 2) * 8) + k
                        c = slice(k * S + hf * 512, k * S + (hf + 1) * 512)
                        dve.wait_ge(h_rounded, 16 * n + i + 1)
                        STT(h_lo[:, c], nbank(n, i), cols[:, g:g + 1], h_hi[:, c].bitcast(F32),
                            ALU.mult, ALU.subtract).then_inc(psum_free, 1)
                    if k == 0:
                        scaled(1)

            link(nc.vector.memset(eps, EPS))
            norm(0)

            dve.wait_ge(pos_in, 32)
            ang, tmp, rs, rc = (scr[:, i * S:(i + 1) * S] for i in (6, 7, 2, 3))
            link(nc.vector.tensor_copy(tmp, pos[:]))
            link(TS(ang, tmp, invf[:], None, ALU.mult))
            parts = (6.28125, 0.00193500518798828125, 3.01991598196e-07)
            for unit in (4096.0, 1.0):
                link(TS(tmp, ang, 1.0 / (6.283185307179586 * unit), None, ALU.mult))
                link(nc.vector.tensor_copy(turns_i[:], tmp))
                link(nc.vector.tensor_copy(tmp, turns_i[:]))
                for part in parts:
                    link(STT(ang, tmp, -part * unit, ang, ALU.mult, ALU.add))
            TS(rs, ang, 3.1415925, -3.1415925, ALU.min, ALU.max).then_inc(table_arg, 1)
            dve.wait_ge(table_arg, 1)
            link(STT(rc, rs, -1.0, rs, ALU.mult, ALU.max))
            TS(rc, rc, -1.0, 1.5707963267948966, ALU.mult, ALU.add).then_inc(table_arg, 1)

            def add(e, le, s, nh):
                c = slice(s * D + nh * 512, s * D + (nh + 1) * 512)
                full(e)
                TT(X[:, c], bank(le), X[:, c], ALU.add).then_inc(psum_free, 1)

            with dve.Fori(0, HEADS) as h:
                base = JB_RET + h * HEAD_JOBS
                step.loop(h, 2)
                dve.wait_ge(rope_in, h * 32 + 32)
                for pair in range(2):
                    n, e, b = h * 8 + pair * 4, base + 4 * pair, 4 * pair
                    cs, sn = (R3[:, 0:512], R3[:, 512:1024]), (R3[:, S:S + 512], R3[:, S + 512:S + 1024])
                    ac, as_, bs, bc = (t(0), t(2)), (t(1), r3(7)), (r3(4), r3(6)), (r3(5), r3(4))
                    dve.wait_ge(psum_full, e + 2)
                    TT(ac[0], bank(b), cs[0], ALU.mult)
                    TT(as_[0], bank(b), sn[0], ALU.mult).then_inc(psum_free, 1)
                    TT(ac[1], bank(b + 2), cs[1], ALU.mult)
                    TT(as_[1], bank(b + 2), sn[1], ALU.mult)
                    dve.wait_ge(psum_full, e + 4)
                    TT(bs[0], bank(b + 1), sn[0], ALU.mult)
                    TT(bc[0], bank(b + 1), cs[0], ALU.mult).then_inc(psum_free, 1)
                    TT(bs[1], bank(b + 3), sn[1], ALU.mult).then_inc(psum_free, 1)
                    dve.wait_ge(psum_free, e + 3)
                    TT(ac[0], ac[0], bs[0], ALU.subtract).then_inc(rope_out, 1)
                    dve.wait_ge(rope_out, n + 1)
                    TT(bc[1], bank(b + 3), cs[1], ALU.mult).then_inc(psum_free, 1)
                    TT(as_[0], bc[0], as_[0], ALU.add).then_inc(rope_out, 1)
                    TT(ac[1], ac[1], bs[1], ALU.subtract).then_inc(rope_out, 1)
                    dve.wait_ge(psum_free, e + 4)
                    TT(as_[1], bc[1], as_[1], ALU.add).then_inc(rope_out, 1)
                    for i in range(4):
                        hf, d = i // 2, i % 2
                        c = slice((2 * pair + d) * S + hf * 512, (2 * pair + d) * S + (hf + 1) * 512)
                        dve.wait_ge(qk_rounded, n + i + 1)
                        TT(a_lo[:, c], (as_ if d else ac)[hf], a_hi[:, c].bitcast(F32), ALU.subtract)\
                            .then_inc(qk_ready, 1)
                    dve.wait_ge(qk_ready, n + 4)
                dve.wait_ge(rope_saved, 32)
                for s in range(SB):
                    dve.wait_ge(g_sig, h * 8 + s + 1)
                    i = TT(r3(s), bank(J_G + s), t(s % 3), ALU.mult)
                    i.then_inc(psum_free, 1)
                dve.wait_ge(decay_in, h * 16 + 16)
                for i in range(len(SCORES) + 1):
                    if i < len(SCORES):
                        c, q, n = SCORES[i]
                        if i >= 3:
                            dve.wait_ge(s_ready, h * 16 + i - 2)
                        else:
                            dve.wait_ge(psum_free, base + J_S)
                        full(base + J_S + i)
                        dst, src, m = T[:, (i % 3) * 512:(i % 3) * 512 + n], bank(J_S + i, 0, n), q // P - c
                        if m == 0:
                            k = TT(dst, src, dk[:, 0:n], ALU.mult)
                        else:
                            k = STT(dst, src, dk[:, 511 + m:512 + m], dk[:, P:P + n], ALU.mult, ALU.mult)
                        k.then_inc(psum_free, 1)
                    if i:
                        n, a = SCORES[i - 1][2], SCORE_AT[i - 1]
                        dve.wait_ge(s_rounded, h * 16 + i)
                        TT(b_lo[:, a:a + n], T[:, ((i - 1) % 3) * 512:((i - 1) % 3) * 512 + n],
                           b_hi[:, a:a + n].bitcast(F32), ALU.subtract).then_inc(s_ready, 1)
                for s in range(SB):
                    dve.wait_ge(v_rounded, h * 8 + s + 1)
                    c = slice(s * 512, (s + 1) * 512)
                    i = TT(a_lo[:, c], bank(J_V + s), a_hi[:, c].bitcast(F32), ALU.subtract)
                    i.then_inc(psum_free, 1)
                def gate_o(blocks):
                    for s in blocks:
                        dve.wait_ge(o_sq, h * 8 + s + 1)
                        TT(r3(s), bank(J_O + s), r3(s), ALU.mult).then_inc(psum_free, 1)

                def mean(hf):
                    q = slice(hf * 4, hf * 4 + 4)
                    TS(ssq[:, q], ssq[:, q], 1.0 / DV, EPS, ALU.mult, ALU.add).then_inc(o_var, 1)

                def norm_o(hf):
                    q = slice(hf * 4, hf * 4 + 4)
                    dve.wait_ge(psum_free, base + J_O + hf * 4 + 4)
                    dve.wait_ge(o_root, 2 * h + hf + 1)
                    link(nc.vector.reciprocal(rstd[:, q], rstd[:, q]))
                    for s in range(hf * 4, hf * 4 + 4):
                        TS(r3(s), r3(s), rstd[:, s:s + 1], None, ALU.mult).then_inc(o_ready, 1)

                gate_o(range(4))
                mean(0)
                gate_o((4,))
                norm_o(0)
                gate_o((5, 6, 7))
                mean(1)
                norm_o(1)
                for s in range(SB):
                    dve.wait_ge(ot_rounded, h * 8 + s + 1)
                    cut = (slice(None), slice(None), slice(s * P, (s + 1) * P))
                    i = TT(b_lo[:, 0:4096].rearrange("p (d n) -> p d n", d=4)[cut],
                           bank(J_T + s).rearrange("p (d n) -> p d n", d=4),
                           b_hi[:, 0:4096].rearrange("p (d n) -> p d n", d=4)[cut].bitcast(F32), ALU.subtract)
                    i.then_inc(psum_free, 1)
                for nh in range(2):
                    for s in range(SB):
                        add(base + J_W + nh * 8 + s, J_W + nh * 8 + s, s, nh)
            step.end(HEADS)

            def ffn(layer):
                def chunk(c, last=False):
                    base, n = JB_FFN[layer] + c * CHUNK_JOBS, (layer * CHUNKS + c) * 4
                    for tile in range(CT):
                        for hf in range(2):
                            i = tile * 2 + hf
                            dve.wait_ge(f_sig, n + i + 1)
                            k = TT(r3(4 + i), bank(4 * tile + 2 * hf), r3(i), ALU.mult)
                            k.then_inc(psum_free, 1)
                            dve.wait_ge(psum_free, base + 4 * tile + 2 * hf + 1)
                            full(base + 4 * tile + 2 + hf)
                            k = TT(r3(4 + i), r3(4 + i), bank(4 * tile + 2 * hf + 1), ALU.mult)
                            k.then_inc(psum_free, 1)
                        for i in (2 * tile, 2 * tile + 1):
                            dve.wait_ge(f_rounded, n + i + 1)
                            at = slice((i // 2) * S + (i % 2) * 512, (i // 2) * S + (i % 2) * 512 + 512)
                            TT(a_lo[:, at], r3(4 + i), a_hi[:, at].bitcast(F32), ALU.subtract)\
                                .then_inc(f_ready, 1)
                    if last:
                        return
                    for nh in range(2):
                        for s in range(SB):
                            add(base + 8 + nh * 8 + s, 8 + nh * 8 + s, s, nh)

                with dve.Fori(0, CHUNKS - layer) as c:
                    chunk(c)
                if layer == 1:
                    chunk(CHUNKS - 1, last=True)

            norm(1)
            lam = cols[:, C_LAM:C_LAM + 12]
            link(TS(small[:, 24:36], lam, -1.0, None, ALU.mult))
            TT(small[:, 0:12], lam, small[:, 24:36], ALU.min).then_inc(lam_e, 1)
            dve.wait_ge(lam_e, 1)
            link(TS(small[:, 24:36], small[:, 24:36], 0.0, None, ALU.max))
            dve.wait_ge(lam_sp, 1)
            z, zz, acc = small[:, 0:12], small[:, 36:48], small[:, 48:60]
            link(TS(z, small[:, 12:24], 2.0, None, ALU.add))
            link(nc.vector.reciprocal(z, z))
            link(TT(z, z, small[:, 12:24], ALU.mult))
            link(TT(zz, z, z, ALU.mult))
            link(TS(acc, zz, 1.0 / 17, 1.0 / 15, ALU.mult, ALU.add))
            for n in (13, 11, 9, 7, 5, 3, 1):
                link(TT(acc, acc, zz, ALU.mult))
                link(TS(acc, acc, 1.0 / n, None, ALU.add))
            link(TT(acc, acc, z, ALU.mult))
            link(STT(acc, acc, 2.0, small[:, 24:36], ALU.mult, ALU.add))
            link(TS(cols[:, C_LAM:C_LAM + 12], acc, 4.0, None, ALU.mult))
            ffn(0)
            norm(2)

            group_cols = cols[:, C_CONV:C_CONV + 96].rearrange("p (q c) -> p q c", q=8)

            def take(dst, g):
                return nc.vector.tensor_copy(dst[:].rearrange("p (q c) -> p q c", q=8),
                                             group_cols[:, :, bass.ds(GT * g, GT)])

            def conv(g, base, e0):
                link(take(gc_conv, g))
                for tile in range(GT):
                    full(base + e0 + 2 * tile + 1)
                    b = (e0 + 2 * tile) % 8 * BANK
                    u = uc[:, tile * S:(tile + 1) * S]

                    def w(j):
                        return gc_conv[:, 3 * j + tile:3 * j + tile + 1]

                    link(TS(u, ps[:, b:b + S], w(3), w(4), ALU.mult, ALU.add))
                    for back in (1, 2, 3):
                        i = STT(u[:, back:], ps[:, b:b + S - back], w(3 - back), u[:, back:], ALU.mult, ALU.add)
                        if back < 3:
                            link(i)
                    i.then_inc(psum_free, 2)

            def gelu_seen(g, e0):
                for tile in range(GT):
                    dve.wait_ge(gelu_done, 3 * g + tile + 1)
                    nc.vector.memset(small[:, 64 + tile:65 + tile], 0.0).then_inc(psum_free, 2)

            def u_split(g, u_hi, u_lo, tiles=range(GT)):
                for tile in tiles:
                    c = slice(tile * S, (tile + 1) * S)
                    dve.wait_ge(u_rounded, 3 * g + tile + 1)
                    TT(u_lo[:, c], uc[:, c], u_hi[:, c].bitcast(F32), ALU.subtract).then_inc(u_ready, 1)

            def gate_chain(g, y_hi, y_lo, meanwhile=lambda blocks: None):
                def cut(i):
                    return slice(i % GT * S + i // GT * 512, i % GT * S + i // GT * 512 + 512)

                def gated(items):
                    for i in items:
                        dve.wait_ge(i_sig, 6 * g + i + 1)
                        TT(uc[:, cut(i)], uc[:, cut(i)], i_buf[i % 3], ALU.mult).then_inc(psum_free, 2)

                def scans(items):
                    first = step.now()
                    for j, i in enumerate(items):
                        dve.wait_ge(a_exp, 6 * g + i + 1)
                        dve.wait_ge(t_root, 6 * g + i + 1)
                        step.up(STT(s_buf[i % 2], r_buf[i % 4], 1.0, s_buf[i % 2], ALU.add, ALU.mult))
                    for j, i in enumerate(items):
                        dve.wait_ge(dve_step, first + j + 1)
                        step.up(TT(uc[:, cut(i)], uc[:, cut(i)], s_buf[i % 2], ALU.mult))
                    for j, i in enumerate(items):
                        dve.wait_ge(dve_step, first + j + 3)
                        tile, hf = i % GT, i // GT
                        start = uc[:, tile * S + 511:tile * S + 512] if hf else 0.0
                        k = nc.vector.tensor_tensor_scan(uc[:, cut(i)], r_buf[i % 4], uc[:, cut(i)], start,
                                                         ALU.mult, ALU.add)
                        k.then_inc(l_scan, 1)
                    for j, i in enumerate(items):
                        dve.wait_ge(l_scan, 6 * g + i + 1)
                        TT(R3[:, cut(i)], uc[:, cut(i)], R3[:, cut(i)], ALU.mult).then_inc(y_out, 1)

                def y_split(items):
                    for i in items:
                        dve.wait_ge(y_rounded, 6 * g + i + 1)
                        TT(y_lo[:, cut(i)], R3[:, cut(i)], y_hi[:, cut(i)].bitcast(F32), ALU.subtract)\
                            .then_inc(y_ready, 1)

                link(take(gc_gate, g))
                TS(gc_gate[:, 0:3], gc_gate[:, 21:24], -2.0, None, ALU.mult).then_inc(gc_ready, 1)
                gated((0, 1))
                scans((0, 1))
                gated((2, 3))
                y_split((0, 1))
                gated((4, 5))
                scans((2, 3))
                meanwhile((0, 1))
                y_split((2, 3))
                meanwhile((2, 3))
                scans((4, 5))
                meanwhile((4,))
                y_split((4, 5))
                meanwhile((5, 6, 7))

            per_turn = 1 + 3 * 3 + 1 + 6 * 2
            conv(0, JB_LRU, 0)
            u_split(0, a_hi, a_lo)
            gelu_seen(0, 6)
            gate_chain(0, a_hi, a_lo)
            with dve.Fori(1, GROUPS - 1) as g:
                base = JB_LRU + L_FIRST + (g - 1) * L_TURN
                step.n -= per_turn
                step.loop(g, per_turn)
                conv(g, base, 0)
                gelu_seen(g, 6)
                for s in range(SB):
                    add(base + L_OUT + s, L_OUT + s, s, 0)
                u_split(g, a_hi, a_lo, (0, 1))
                for s in range(SB):
                    add(base + L_OUT + 8 + s, L_OUT + 8 + s, s, 1)
                u_split(g, a_hi, a_lo, (2,))
                gate_chain(g, a_hi, a_lo)
            step.end(GROUPS - 1)

            base = JB_LRU + L_FIRST + (GROUPS - 2) * L_TURN
            conv(GROUPS - 1, base, 0)
            gelu_seen(GROUPS - 1, 6)
            u_split(GROUPS - 1, h_hi, h_lo)
            for s in range(SB):
                add(base + L_OUT + s, L_OUT + s, s, 0)

            def second_half_out(blocks):
                for s in blocks:
                    add(base + L_RI_LAST + 12 + s, L_RI_LAST + 12 + s, s, 1)

            gate_chain(GROUPS - 1, h_hi, h_lo, second_half_out)
            for nh in range(2):
                for s in range(SB):
                    add(base + L_TURN + nh * 8 + s, nh * 8 + s, s, nh)
            norm(3)
            ffn(1)
            fn = scr[:, 0:D]

            def final(s):
                turn = norm_turns(4)[s][2]
                dve.wait_ge(n_root, turn)
                nc.vector.reciprocal(rstd[:, s:s + 1], rstd[:, s:s + 1]).then_inc(n_rstd, 1)
                dve.wait_ge(n_rstd, turn)
                STT(X[:, s * D:(s + 1) * D], X[:, s * D:(s + 1) * D], rstd[:, s:s + 1], fn,
                    ALU.mult, ALU.mult).then_inc(out_ready, 1)

            dve.wait_ge(fn_in, 16)
            for s in range(SB):
                for nh in range(2):
                    e = JOBS - 16 + 2 * s + nh
                    add(e, e, s, nh)
                if s:
                    final(s - 1)
            final(SB - 1)


INS = ["x", "positions", "mix_norm", "ffn_norm", "final_norm", "ret_w_in", "ret_w_out", "lru_w_in",
       "lru_conv_w", "lru_conv_b", "lru_w_r", "lru_b_r", "lru_w_i", "lru_b_i", "lru_lambda", "lru_w_out",
       "ffn_w_gu", "ffn_w_down"]


def constants():
    import numpy as np
    freq = np.float32(10000.0) ** (-np.arange(P, dtype=np.float32) * np.float32(2.0) / np.float32(DK))
    log_gamma = np.log1p(-(2.0 ** (-5.0 - np.arange(HEADS, dtype=np.float64))))
    rel = np.arange(BANK, dtype=np.float64)[None, :] - np.arange(P, dtype=np.float64)[:, None]
    table = np.where(rel >= 0, np.exp(np.maximum(rel, 0.0) * log_gamma[:, None, None]), 0.0) * DK ** -0.5
    blocks = np.exp(P * np.arange(8)[None, None, :] * log_gamma[:, None, None]) * np.ones((1, P, 1))
    table = np.concatenate([table, blocks], axis=2)
    return {"inv_freq": freq.reshape(P, 1).astype(np.float32), "decay": table.astype(np.float32)}


def kernel(**inputs):
    import numpy as np
    import concourse.bacc as bacc
    from concourse.bass_utils import run_bass_kernel_spmd

    nc = bacc.Bacc("TRN2", target_bir_lowering=False, num_devices=1)
    arrays, args = {}, []
    given = {name: np.ascontiguousarray(inputs[name]) for name in INS}
    for name, a in {**given, **constants()}.items():
        arrays[f"in_{name}"] = a
        args.append(nc.dram_tensor(f"in_{name}", a.shape, mybir.dt.from_np(a.dtype), kind="ExternalInput").ap())
    y = nc.dram_tensor("out_y", (1, S, D), F32, kind="ExternalOutput").ap()
    build(nc, *args, y)
    r = run_bass_kernel_spmd(nc, [arrays], core_ids=[0])
    return r.results[0]["out_y"]
```
